# Optimizing a Trainium2 kernel written in Bass

```python
import math
import jax, jax.numpy as jnp
from jax import lax
import numpy as np

D_MODEL = 1024
BATCH = 1
SEQ = 256
DEPTH = 1

A_HEADS = 8
A_HEAD_DIM = 64
A_WIDTH = A_HEADS * A_HEAD_DIM
DILATED_PATTERNS = ((128, 1), (512, 4), (2048, 16))
BAND_BLOCK = 128
REL_BUCKETS = 32
REL_MAX_DIST = 2048
M_HEADS = 8
M_NOPE = 64
M_ROPE = 32
M_V = 64
M_Q_LORA = 768
M_KV_LORA = 256
M_WIDTH = M_HEADS * M_V
ROPE_THETA = 10000.0
Q_BLOCK = 128
D_FF = -(-8 * D_MODEL // (3 * 256)) * 256
N_MOD = 6
EPS = 1e-6
NEG_INF = -1e30
IN_SIZES = (3 * A_WIDTH, M_Q_LORA, M_KV_LORA, M_ROPE, D_MODEL, D_MODEL)
IN_WIDTH = 3 * A_WIDTH + M_Q_LORA + M_KV_LORA + M_ROPE + 2 * D_MODEL
IN_SPLIT_POINTS = (3 * A_WIDTH,
                   3 * A_WIDTH + M_Q_LORA,
                   3 * A_WIDTH + M_Q_LORA + M_KV_LORA,
                   3 * A_WIDTH + M_Q_LORA + M_KV_LORA + M_ROPE,
                   3 * A_WIDTH + M_Q_LORA + M_KV_LORA + M_ROPE + D_MODEL)


def _rmsnorm(x, g):
    xf = x.astype(jnp.float32)
    inv = lax.rsqrt(jnp.mean(xf * xf, axis=-1, keepdims=True) + EPS)
    return (xf * inv).astype(x.dtype) * g

def _t5_bucket(dist):
    max_exact = REL_BUCKETS // 2
    d = jnp.maximum(dist, 1).astype(jnp.float32)
    log_b = max_exact + (jnp.log(d / max_exact) / math.log(REL_MAX_DIST / max_exact)
                         * (REL_BUCKETS - max_exact)).astype(jnp.int32)
    log_b = jnp.minimum(log_b, REL_BUCKETS - 1)
    return jnp.where(dist < max_exact, dist, log_b)

def _dilated_pattern(q, k, v, rel_bias, window, dilation):
    B, H, S, Dh = q.shape
    n_back = window // dilation
    blk = BAND_BLOCK
    L = S // dilation
    pad_end = (-L) % blk
    Lp = L + pad_end
    nb = Lp // blk

    def to_sub(t):
        t = t.reshape(B, H, L, dilation, Dh).transpose(0, 1, 3, 2, 4)
        return jnp.pad(t, ((0, 0), (0, 0), (0, 0), (0, pad_end), (0, 0)))

    def band(t):
        tp = jnp.pad(t, ((0, 0), (0, 0), (0, 0), (blk, 0), (0, 0)))
        prev = tp[:, :, :, :Lp].reshape(B, H, dilation, nb, blk, Dh)
        cur = t.reshape(B, H, dilation, nb, blk, Dh)
        return jnp.concatenate([prev, cur], axis=4)

    qb = to_sub(q).reshape(B, H, dilation, nb, blk, Dh)
    kb = band(to_sub(k))
    vb = band(to_sub(v))
    s = jnp.einsum('bhrnqd,bhrnkd->bhrnqk', qb, kb).astype(jnp.float32) * (Dh ** -0.5)
    sub_dist = (jnp.arange(blk)[:, None] + blk) - jnp.arange(2 * blk)[None, :]
    in_band = (sub_dist >= 0) & (sub_dist <= n_back)
    bucket = _t5_bucket(jnp.clip(sub_dist, 0, n_back) * dilation)
    bias = rel_bias[:, bucket].astype(jnp.float32)
    key_idx = jnp.arange(nb)[:, None] * blk + jnp.arange(2 * blk)[None, :] - blk
    mask = in_band[None] & (key_idx >= 0)[:, None, :]
    s = jnp.where(mask, s + bias[None, :, None, None], NEG_INF)
    lse = jax.nn.logsumexp(s, axis=-1)
    p = jnp.exp(s - lse[..., None])
    o = jnp.einsum('bhrnqk,bhrnkd->bhrnqd', p.astype(v.dtype), vb)
    o = o.reshape(B, H, dilation, Lp, Dh)[:, :, :, :L].transpose(0, 1, 3, 2, 4).reshape(B, H, S, Dh)
    lse = lse.reshape(B, H, dilation, Lp)[:, :, :, :L].transpose(0, 1, 3, 2).reshape(B, H, S)
    return o, lse

def _dilated_attention(a_qkv, rel_bias):
    B, S, _ = a_qkv.shape
    qkv = a_qkv.reshape(B, S, 3, A_HEADS, A_HEAD_DIM).transpose(2, 0, 3, 1, 4)
    q, k, v = qkv[0], qkv[1], qkv[2]
    outs, lses = [], []
    for window, dilation in DILATED_PATTERNS:
        o, l = _dilated_pattern(q, k, v, rel_bias, window, dilation)
        outs.append(o)
        lses.append(l)
    w = jax.nn.softmax(jnp.stack(lses), axis=0)
    o = jnp.einsum('gbhs,gbhsd->bhsd', w.astype(v.dtype), jnp.stack(outs))
    return o.transpose(0, 2, 1, 3).reshape(B, S, A_WIDTH)

def _rope(x, pos):
    half = x.shape[-1] // 2
    freqs = ROPE_THETA ** (-jnp.arange(half, dtype=jnp.float32) / half)
    ang = pos.astype(jnp.float32)[..., None] * freqs
    ang = ang.reshape(ang.shape[:2] + (1,) * (x.ndim - 3) + (half,))
    cos, sin = jnp.cos(ang), jnp.sin(ang)
    x1 = x[..., :half].astype(jnp.float32)
    x2 = x[..., half:].astype(jnp.float32)
    return jnp.concatenate([x1 * cos - x2 * sin, x1 * sin + x2 * cos], axis=-1).astype(x.dtype)

def _mla(c_q, c_kv, k_r, positions, g_q_lora, w_uq, g_kv_lora, w_ukv):
    B, S, _ = c_q.shape
    q = jnp.einsum('bsl,lhd->bshd', _rmsnorm(c_q, g_q_lora), w_uq)
    kv = jnp.einsum('bsl,lhd->bshd', _rmsnorm(c_kv, g_kv_lora), w_ukv)
    q_nope, q_rope = q[..., :M_NOPE], _rope(q[..., M_NOPE:], positions)
    k_nope, v = kv[..., :M_NOPE], kv[..., M_NOPE:]
    k_rope = _rope(k_r, positions)
    scale = (M_NOPE + M_ROPE) ** -0.5
    nq = S // Q_BLOCK
    qn_b = jnp.moveaxis(q_nope.reshape(B, nq, Q_BLOCK, M_HEADS, M_NOPE), 1, 0)
    qr_b = jnp.moveaxis(q_rope.reshape(B, nq, Q_BLOCK, M_HEADS, M_ROPE), 1, 0)
    kpos = jnp.arange(S)

    def block(args):
        qn, qr, i = args
        s = (jnp.einsum('bqhd,bkhd->bhqk', qn, k_nope)
             + jnp.einsum('bqhr,bkr->bhqk', qr, k_rope)).astype(jnp.float32) * scale
        qpos = i * Q_BLOCK + jnp.arange(Q_BLOCK)
        s = jnp.where(kpos[None, :] <= qpos[:, None], s, NEG_INF)
        p = jax.nn.softmax(s, axis=-1)
        return jnp.einsum('bhqk,bkhd->bqhd', p.astype(v.dtype), v)

    o = lax.map(block, (qn_b, qr_b, jnp.arange(nq)))
    return jnp.moveaxis(o, 0, 1).reshape(B, S, M_WIDTH)

def _hybrid_mixer(h, positions, rel_bias, w_in, g_q_lora, w_uq, g_kv_lora, w_ukv,
                  w_up_a, w_up_b, w_o):
    proj = h @ w_in
    a_qkv, c_q, c_kv, k_r, gate_a, gate_b = jnp.split(proj, IN_SPLIT_POINTS, axis=-1)
    y_a = _dilated_attention(a_qkv, rel_bias) @ w_up_a
    y_b = _mla(c_q, c_kv, k_r, positions, g_q_lora, w_uq, g_kv_lora, w_ukv) @ w_up_b
    merged = jax.nn.sigmoid(gate_a) * y_a + jax.nn.sigmoid(gate_b) * y_b
    return merged @ w_o

def _swiglu(h, w_gate, w_up, w_down):
    return (jax.nn.silu(h @ w_gate) * (h @ w_up)) @ w_down

def first_inputs(seed: int = 0) -> dict:
    key = jax.random.key(seed)
    ks = jax.random.split(key, 20)
    f32 = jnp.float32

    def nrm(k, shape, fan_in, mult=1.0):
        return jax.random.normal(k, shape, f32) * (mult * fan_in ** -0.5)

    def gain(k, shape):
        return 1.0 + 0.05 * jax.random.normal(k, shape, f32)

    x = jax.random.normal(ks[0], (BATCH, SEQ, D_MODEL), f32)
    c = jax.random.normal(ks[1], (BATCH, D_MODEL), f32)
    offsets = jax.random.randint(ks[2], (BATCH, 1), 0, 4096, dtype=jnp.int32)
    positions = offsets + jnp.arange(SEQ, dtype=jnp.int32)[None, :]
    return {
        "x": x,
        "c": c,
        "positions": positions,
        "rel_bias": 0.5 * jax.random.normal(ks[3], (A_HEADS, REL_BUCKETS), f32),
        "w_ada": nrm(ks[4], (DEPTH, D_MODEL, N_MOD * D_MODEL), D_MODEL, 0.5),
        "b_ada": 0.02 * jax.random.normal(ks[5], (DEPTH, N_MOD * D_MODEL), f32),
        "g_mix": gain(ks[6], (DEPTH, D_MODEL)),
        "w_in": nrm(ks[7], (DEPTH, D_MODEL, IN_WIDTH), D_MODEL),
        "g_q_lora": gain(ks[8], (DEPTH, M_Q_LORA)),
        "w_uq": nrm(ks[9], (DEPTH, M_Q_LORA, M_HEADS, M_NOPE + M_ROPE), M_Q_LORA),
        "g_kv_lora": gain(ks[10], (DEPTH, M_KV_LORA)),
        "w_ukv": nrm(ks[11], (DEPTH, M_KV_LORA, M_HEADS, M_NOPE + M_V), M_KV_LORA),
        "w_up_a": nrm(ks[12], (DEPTH, A_WIDTH, D_MODEL), A_WIDTH),
        "w_up_b": nrm(ks[13], (DEPTH, M_WIDTH, D_MODEL), M_WIDTH),
        "w_o": nrm(ks[14], (DEPTH, D_MODEL, D_MODEL), D_MODEL),
        "g_ffn": gain(ks[15], (DEPTH, D_MODEL)),
        "w_gate": nrm(ks[16], (DEPTH, D_MODEL, D_FF), D_MODEL),
        "w_up": nrm(ks[17], (DEPTH, D_MODEL, D_FF), D_MODEL),
        "w_down": nrm(ks[18], (DEPTH, D_FF, D_MODEL), D_FF),
        "g_final": gain(ks[19], (D_MODEL,)),
    }

def first_block(x, c, positions, rel_bias, w_ada, b_ada, g_mix, w_in, g_q_lora, w_uq,
              g_kv_lora, w_ukv, w_up_a, w_up_b, w_o, g_ffn, w_gate, w_up, w_down, g_final):
    cond = jax.nn.silu(c)
    for layer in range(DEPTH):
        mod = (cond @ w_ada[layer] + b_ada[layer])[:, None, :]
        sh1, sc1, gt1, sh2, sc2, gt2 = jnp.split(mod, N_MOD, axis=-1)
        h = _rmsnorm(x, g_mix[layer]) * (1.0 + sc1) + sh1
        x = x + gt1 * _hybrid_mixer(h, positions, rel_bias, w_in[layer], g_q_lora[layer],
                                    w_uq[layer], g_kv_lora[layer], w_ukv[layer],
                                    w_up_a[layer], w_up_b[layer], w_o[layer])
        h = _rmsnorm(x, g_ffn[layer]) * (1.0 + sc2) + sh2
        x = x + gt2 * _swiglu(h, w_gate[layer], w_up[layer], w_down[layer])
    return _rmsnorm(x, g_final)


D_MIX = D_MODEL
N_GROUPS = 4
GROUP = D_MIX // N_GROUPS
HEAD_DIM = 64
LRU_BLOCKS = GROUP // HEAD_DIM
LRU_BLOCK_DIM = GROUP // LRU_BLOCKS
LRU_CONV = 4
LRU_C = 8.0
SC_CONV = 3
FOX_HEADS = GROUP // HEAD_DIM
NSA_HEADS = GROUP // HEAD_DIM
CMP_LEN = 32
CMP_STRIDE = 16
CMP_HIDDEN = 128
SLC_BLOCK = 64
SLC_TOPK = 16
WINDOW = 512
REL_MAX_DIST_2 = 128
D_FF_2 = ((8 * D_MODEL // 3 + 255) // 256) * 256
NEG_INF_2 = -1e30
BIG = 1e30
RMS_EPS = 1e-6

C_LRU_X = 0
C_LRU_G = C_LRU_X + GROUP
C_SC_B = C_LRU_G + GROUP
C_SC_C = C_SC_B + GROUP
C_SC_X = C_SC_C + GROUP
C_FOX_Q = C_SC_X + GROUP
C_FOX_K = C_FOX_Q + GROUP
C_FOX_V = C_FOX_K + GROUP
C_FOX_F = C_FOX_V + GROUP
C_NSA_Q = C_FOX_F + FOX_HEADS
C_NSA_KV = C_NSA_Q + GROUP
C_NSA_G = C_NSA_KV + 6 * HEAD_DIM
N_IN = C_NSA_G + 3 * NSA_HEADS


def rms_norm(x, g):
    xf = x.astype(jnp.float32)
    y = xf * lax.rsqrt(jnp.mean(xf * xf, axis=-1, keepdims=True) + RMS_EPS)
    return (y * g.astype(jnp.float32)).astype(x.dtype)

def cols(z, start, width):
    return z[..., start:start + width]

def causal_dwconv(x, w):
    k_len, ch = w.shape
    return lax.conv_general_dilated(x, w[:, None, :], window_strides=(1,), padding=[(k_len - 1, 0)],
                                    dimension_numbers=('NWC', 'WIO', 'NWC'), feature_group_count=ch)

def masked_softmax(s, mask):
    p = jax.nn.softmax(jnp.where(mask, s, NEG_INF_2), axis=-1)
    return jnp.where(mask, p, 0.0)

def rel_bucket(dist):
    max_exact = REL_BUCKETS // 2
    d = jnp.maximum(dist, 0)
    large = max_exact + (jnp.log(jnp.maximum(d, 1).astype(jnp.float32) / max_exact)
                         / math.log(REL_MAX_DIST_2 / max_exact) * (REL_BUCKETS - max_exact)).astype(jnp.int32)
    large = jnp.minimum(large, REL_BUCKETS - 1)
    return jnp.where(d < max_exact, d, large)

def rg_lru_mixer(xr, gate, conv_w, conv_b, w_gates, b_gates, lam):
    bsz, s_len, _ = xr.shape
    xc = causal_dwconv(xr, conv_w) + conv_b
    xb = xc.reshape(bsz, s_len, LRU_BLOCKS, LRU_BLOCK_DIM)
    r = jax.nn.sigmoid(jnp.einsum('bshi,hij->bshj', xb, w_gates[0]).reshape(bsz, s_len, GROUP) + b_gates[0])
    i = jax.nn.sigmoid(jnp.einsum('bshi,hij->bshj', xb, w_gates[1]).reshape(bsz, s_len, GROUP) + b_gates[1])
    log_a = (-LRU_C * jax.nn.softplus(-lam.astype(jnp.float32))) * r.astype(jnp.float32)
    a = jnp.exp(log_a)
    b = jnp.sqrt(-jnp.expm1(2.0 * log_a)) * (i * xc).astype(jnp.float32)

    def combine(left, right):
        a1, b1 = left
        a2, b2 = right
        return a1 * a2, a2 * b1 + b2

    _, h = lax.associative_scan(combine, (a, b), axis=1)
    return h.astype(xr.dtype) * jax.nn.gelu(gate)

def short_conv_mixer(bg, cg, xs, conv_w):
    return bg * causal_dwconv(cg * xs, conv_w)

def fox_mixer(q, k, v, f_logit, f_bias, qk_gain):
    bsz, s_len, _ = q.shape
    h, d = FOX_HEADS, HEAD_DIM
    q = rms_norm(q.reshape(bsz, s_len, h, d), qk_gain[0])
    k = rms_norm(k.reshape(bsz, s_len, h, d), qk_gain[1])
    v = v.reshape(bsz, s_len, h, d)
    logf = jax.nn.log_sigmoid((f_logit + f_bias).astype(jnp.float32))
    c = lax.cumsum(logf, axis=1).transpose(0, 2, 1)
    nb = s_len // Q_BLOCK
    qb = q.reshape(bsz, nb, Q_BLOCK, h, d).swapaxes(0, 1)
    cb = c.reshape(bsz, h, nb, Q_BLOCK).transpose(2, 0, 1, 3)
    kpos = jnp.arange(s_len)
    scale = HEAD_DIM ** -0.5

    def block(args):
        qi, ci, bi = args
        t = bi * Q_BLOCK + jnp.arange(Q_BLOCK)
        s = jnp.einsum('bqhd,bkhd->bhqk', qi, k).astype(jnp.float32) * scale + (ci[..., :, None] - c[..., None, :])
        p = masked_softmax(s, kpos[None, :] <= t[:, None])
        return jnp.einsum('bhqk,bkhd->bqhd', p.astype(v.dtype), v)

    o = lax.map(block, (qb, cb, jnp.arange(nb)))
    return o.swapaxes(0, 1).reshape(bsz, s_len, GROUP)

def compress(kx, pos, w1, w2):
    s_len = kx.shape[1]
    n_cmp = (s_len - CMP_LEN) // CMP_STRIDE + 1
    idx = jnp.arange(n_cmp)[:, None] * CMP_STRIDE + jnp.arange(CMP_LEN)[None, :]
    blocks = kx[:, idx] + pos
    hid = jax.nn.gelu(jnp.einsum('bnld,ldm->bnm', blocks, w1))
    return hid @ w2

def nsa_mixer(q, kc_in, vc_in, ks_in, vs_in, kw_in, vw_in, g_logit, g_bias, qk_gain, cmp_pos, cmp_w1, cmp_w2, rel_bias):
    bsz, s_len, _ = q.shape
    h, d = NSA_HEADS, HEAD_DIM
    f32 = jnp.float32
    q = rms_norm(q.reshape(bsz, s_len, h, d), qk_gain[0])
    kc = rms_norm(compress(kc_in, cmp_pos[0], cmp_w1[0], cmp_w2[0]), qk_gain[1])
    vc = compress(vc_in, cmp_pos[1], cmp_w1[1], cmp_w2[1])
    ks_ = rms_norm(ks_in, qk_gain[2])
    kw = rms_norm(kw_in, qk_gain[3])
    gates = jax.nn.sigmoid(g_logit + g_bias).reshape(bsz, s_len, 3, h)
    n_cmp = kc.shape[1]
    n_slc = s_len // SLC_BLOCK
    top = min(SLC_TOPK, n_slc)
    cmp_start = jnp.arange(n_cmp) * CMP_STRIDE
    cmp_end = cmp_start + CMP_LEN - 1
    slc_start = jnp.arange(n_slc) * SLC_BLOCK
    overlap = jnp.clip(jnp.minimum(cmp_start[:, None] + CMP_LEN, slc_start[None, :] + SLC_BLOCK)
                       - jnp.maximum(cmp_start[:, None], slc_start[None, :]), 0, CMP_LEN).astype(f32)
    ks_blk = ks_.reshape(bsz, n_slc, SLC_BLOCK, d)
    vs_blk = vs_in.reshape(bsz, n_slc, SLC_BLOCK, d)
    kw_pad = jnp.pad(kw, ((0, 0), (WINDOW, 0), (0, 0)))
    vw_pad = jnp.pad(vw_in, ((0, 0), (WINDOW, 0), (0, 0)))
    nb = s_len // Q_BLOCK
    qb = q.reshape(bsz, nb, Q_BLOCK, h, d).swapaxes(0, 1)
    gb = gates.reshape(bsz, nb, Q_BLOCK, 3, h).swapaxes(0, 1)
    bidx = jnp.arange(bsz)[:, None, None]
    jblk = jnp.arange(n_slc)
    scale = HEAD_DIM ** -0.5

    def block(args):
        qi, gi, bi = args
        t = bi * Q_BLOCK + jnp.arange(Q_BLOCK)
        dist_c = t[:, None] - cmp_end[None, :]
        s_c = (jnp.einsum('bqhd,bnd->bhqn', qi, kc).astype(f32) * scale
               + rel_bias[rel_bucket(dist_c)].transpose(2, 0, 1))
        p_c = masked_softmax(s_c, dist_c >= 0)
        o_c = jnp.einsum('bhqn,bnd->bqhd', p_c.astype(vc.dtype), vc)
        imp = jnp.einsum('bhqn,nm->bqm', p_c, overlap)
        cur = t // SLC_BLOCK
        forced = (jblk[None, :] == 0) | (jblk[None, :] == cur[:, None]) | (jblk[None, :] == cur[:, None] - 1)
        imp = jnp.where(forced, BIG, imp)
        imp = jnp.where(jblk[None, :] <= cur[:, None], imp, -jnp.inf)
        _, sel = lax.top_k(imp, top)
        k_sel = ks_blk[bidx, sel].reshape(bsz, Q_BLOCK, top * SLC_BLOCK, d)
        v_sel = vs_blk[bidx, sel].reshape(bsz, Q_BLOCK, top * SLC_BLOCK, d)
        pos_sel = (sel[..., None] * SLC_BLOCK + jnp.arange(SLC_BLOCK)).reshape(bsz, Q_BLOCK, top * SLC_BLOCK)
        dist_s = t[None, :, None] - pos_sel
        s_s = (jnp.einsum('bqhd,bqnd->bhqn', qi, k_sel).astype(f32) * scale
               + rel_bias[rel_bucket(dist_s)].transpose(0, 3, 1, 2))
        p_s = masked_softmax(s_s, (dist_s >= 0)[:, None])
        o_s = jnp.einsum('bhqn,bqnd->bqhd', p_s.astype(v_sel.dtype), v_sel)
        k_win = lax.dynamic_slice_in_dim(kw_pad, bi * Q_BLOCK, WINDOW + Q_BLOCK, axis=1)
        v_win = lax.dynamic_slice_in_dim(vw_pad, bi * Q_BLOCK, WINDOW + Q_BLOCK, axis=1)
        pos_w = bi * Q_BLOCK - WINDOW + jnp.arange(WINDOW + Q_BLOCK)
        dist_w = t[:, None] - pos_w[None, :]
        mask_w = (dist_w >= 0) & (dist_w < WINDOW) & (pos_w[None, :] >= 0)
        s_w = (jnp.einsum('bqhd,bnd->bhqn', qi, k_win).astype(f32) * scale
               + rel_bias[rel_bucket(dist_w)].transpose(2, 0, 1))
        p_w = masked_softmax(s_w, mask_w)
        o_w = jnp.einsum('bhqn,bnd->bqhd', p_w.astype(v_win.dtype), v_win)
        return gi[:, :, 0, :, None] * o_c + gi[:, :, 1, :, None] * o_s + gi[:, :, 2, :, None] * o_w

    o = lax.map(block, (qb, gb, jnp.arange(nb)))
    return o.swapaxes(0, 1).reshape(bsz, s_len, GROUP)

def second_inputs(seed: int = 0) -> dict:
    key = jax.random.key(seed)
    ks = jax.random.split(key, 24)
    f32 = jnp.float32
    nl = DEPTH

    def nrm(k, shape, scale):
        return jax.random.normal(k, shape, f32) * scale

    u = jax.random.uniform(ks[7], (nl, GROUP), f32, 0.9, 0.999)
    return {
        'x': jax.random.normal(ks[0], (BATCH, SEQ, D_MODEL), f32),
        'norm_mix': 1.0 + nrm(ks[1], (nl, D_MODEL), 0.02),
        'w_in': nrm(ks[2], (nl, D_MODEL, N_IN), D_MODEL ** -0.5),
        'lru_conv_w': nrm(ks[3], (nl, LRU_CONV, GROUP), LRU_CONV ** -0.5),
        'lru_conv_b': nrm(ks[4], (nl, GROUP), 0.02),
        'lru_w_gates': nrm(ks[5], (nl, 2, LRU_BLOCKS, LRU_BLOCK_DIM, LRU_BLOCK_DIM), LRU_BLOCK_DIM ** -0.5),
        'lru_b_gates': nrm(ks[6], (nl, 2, GROUP), 0.02),
        'lru_lambda': jnp.log(u) - jnp.log1p(-u),
        'sc_conv_w': nrm(ks[8], (nl, SC_CONV, GROUP), SC_CONV ** -0.5),
        'fox_f_bias': 3.0 + nrm(ks[9], (nl, FOX_HEADS), 0.1),
        'fox_qk_norm': 1.0 + nrm(ks[10], (nl, 2, HEAD_DIM), 0.02),
        'nsa_qk_norm': 1.0 + nrm(ks[11], (nl, 4, HEAD_DIM), 0.02),
        'nsa_cmp_pos': nrm(ks[12], (nl, 2, CMP_LEN, HEAD_DIM), 0.1),
        'nsa_cmp_w1': nrm(ks[13], (nl, 2, CMP_LEN, HEAD_DIM, CMP_HIDDEN), (CMP_LEN * HEAD_DIM) ** -0.5),
        'nsa_cmp_w2': nrm(ks[14], (nl, 2, CMP_HIDDEN, HEAD_DIM), CMP_HIDDEN ** -0.5),
        'nsa_gate_bias': nrm(ks[15], (nl, 3 * NSA_HEADS), 0.02),
        'rel_bias': nrm(ks[16], (REL_BUCKETS, NSA_HEADS), 0.2),
        'out_norm': 1.0 + nrm(ks[17], (nl, N_GROUPS, GROUP), 0.02),
        'w_out': nrm(ks[18], (nl, D_MIX, D_MODEL), D_MIX ** -0.5),
        'norm_ffn': 1.0 + nrm(ks[19], (nl, D_MODEL), 0.02),
        'w_gate_up': nrm(ks[20], (nl, D_MODEL, 2 * D_FF_2), D_MODEL ** -0.5),
        'w_down': nrm(ks[21], (nl, D_FF_2, D_MODEL), D_FF_2 ** -0.5),
    }

def second_block(x, norm_mix, w_in, lru_conv_w, lru_conv_b, lru_w_gates, lru_b_gates, lru_lambda, sc_conv_w,
              fox_f_bias, fox_qk_norm, nsa_qk_norm, nsa_cmp_pos, nsa_cmp_w1, nsa_cmp_w2, nsa_gate_bias,
              rel_bias, out_norm, w_out, norm_ffn, w_gate_up, w_down):
    for l in range(DEPTH):
        z = rms_norm(x, norm_mix[l]) @ w_in[l]
        y_a = rg_lru_mixer(cols(z, C_LRU_X, GROUP), cols(z, C_LRU_G, GROUP), lru_conv_w[l], lru_conv_b[l],
                           lru_w_gates[l], lru_b_gates[l], lru_lambda[l])
        y_b = short_conv_mixer(cols(z, C_SC_B, GROUP), cols(z, C_SC_C, GROUP), cols(z, C_SC_X, GROUP), sc_conv_w[l])
        y_c = fox_mixer(cols(z, C_FOX_Q, GROUP), cols(z, C_FOX_K, GROUP), cols(z, C_FOX_V, GROUP),
                        cols(z, C_FOX_F, FOX_HEADS), fox_f_bias[l], fox_qk_norm[l])
        kv = [cols(z, C_NSA_KV + j * HEAD_DIM, HEAD_DIM) for j in range(6)]
        y_d = nsa_mixer(cols(z, C_NSA_Q, GROUP), kv[0], kv[1], kv[2], kv[3], kv[4], kv[5],
                        cols(z, C_NSA_G, 3 * NSA_HEADS), nsa_gate_bias[l], nsa_qk_norm[l],
                        nsa_cmp_pos[l], nsa_cmp_w1[l], nsa_cmp_w2[l], rel_bias)
        mixed = jnp.concatenate([rms_norm(y_a, out_norm[l, 0]), rms_norm(y_b, out_norm[l, 1]),
                                 rms_norm(y_c, out_norm[l, 2]), rms_norm(y_d, out_norm[l, 3])], axis=-1)
        x = x + mixed @ w_out[l]
        gu = rms_norm(x, norm_ffn[l]) @ w_gate_up[l]
        x = x + (jax.nn.silu(gu[..., :D_FF_2]) * gu[..., D_FF_2:]) @ w_down[l]
    return x


def setup_inputs(seed=0):
    out = dict(first_inputs(seed))
    for name, value in second_inputs(seed + 1).items():
        if name != "x":
            out[name + "_2"] = value
    return out


def reference(
    x, c, positions, rel_bias, w_ada, b_ada, g_mix, w_in, g_q_lora, w_uq, g_kv_lora, w_ukv,
    w_up_a, w_up_b, w_o, g_ffn, w_gate, w_up, w_down, g_final, norm_mix_2, w_in_2, lru_conv_w_2,
    lru_conv_b_2, lru_w_gates_2, lru_b_gates_2, lru_lambda_2, sc_conv_w_2, fox_f_bias_2,
    fox_qk_norm_2, nsa_qk_norm_2, nsa_cmp_pos_2, nsa_cmp_w1_2, nsa_cmp_w2_2, nsa_gate_bias_2,
    rel_bias_2, out_norm_2, w_out_2, norm_ffn_2, w_gate_up_2, w_down_2,
):
    x = first_block(
        x, c, positions, rel_bias, w_ada, b_ada, g_mix, w_in, g_q_lora, w_uq, g_kv_lora, w_ukv,
        w_up_a, w_up_b, w_o, g_ffn, w_gate, w_up, w_down, g_final,
    )
    return second_block(
        x, norm_mix_2, w_in_2, lru_conv_w_2, lru_conv_b_2, lru_w_gates_2, lru_b_gates_2,
        lru_lambda_2, sc_conv_w_2, fox_f_bias_2, fox_qk_norm_2, nsa_qk_norm_2, nsa_cmp_pos_2,
        nsa_cmp_w1_2, nsa_cmp_w2_2, nsa_gate_bias_2, rel_bias_2, out_norm_2, w_out_2,
        norm_ffn_2, w_gate_up_2, w_down_2,
    )


_drawn_inputs = setup_inputs


def setup_inputs(seed=0):
    import zlib

    import numpy as np

    out = dict(_drawn_inputs(seed))
    spreads = {}
    factors = {'rel_bias': 2.682,
     'g_mix': 6.827,
     'g_q_lora': 8.0,
     'g_kv_lora': 7.329,
     'lru_b_gates_2': 8.0,
     'fox_f_bias_2': 30.888,
     'fox_qk_norm_2': 6.251,
     'nsa_qk_norm_2': 7.085,
     'nsa_gate_bias_2': 8.0,
     'out_norm_2': 3.675,
     'norm_ffn_2': 4.633,
     'rel_bias_2': 3.49}
    for name, (base, spread) in spreads.items():
        noise = np.random.default_rng([zlib.crc32(name.encode()), seed]).standard_normal(out[name].shape)
        drawn = base * np.exp(spread * noise) if base else spread * noise
        out[name] = __import__('jax').numpy.asarray(drawn.astype(out[name].dtype))
    for name, factor in factors.items():
        out[name] = (out[name] * factor).astype(out[name].dtype)
    return out
```

```python
import math
from contextlib import ExitStack

import numpy as np

import concourse.bass as bass
from concourse import mybir

P = 128
SEQ = 256
TT = SEQ // P
D = 1024
KC = D // P
A_HEADS, HD = 8, 64
AW = A_HEADS * HD
Q_LORA, KV_LORA, ROPE = 768, 256, 32
HALF = ROPE // 2
MH, NOPE, MV = 8, 64, 64
MQ = NOPE + ROPE
D_FF = -(-8 * D // (3 * 256)) * 256
FC = D_FF // P
GROUP = D // 4
FOX_HEADS = NSA_HEADS = GROUP // HD
CMP_LEN, CMP_STRIDE = 32, 16
NCMP = (SEQ - CMP_LEN) // CMP_STRIDE + 1
NCMP0 = (P - CMP_LEN) // CMP_STRIDE + 1
BUCKETS = 32
NEG = -1e30
EPS = 1e-6
SCALE = HD ** -0.5
M_SCALE = MQ ** -0.5
FW = 384
NB = A_HEADS + NSA_HEADS

C_CQ = 3 * AW
C_KV = C_CQ + Q_LORA
C_KR = C_KV + KV_LORA
C_GA = C_KR + ROPE
C_GB = C_GA + D
C_LX, C_LG, C_SB, C_SC, C_SX, C_FQ, C_FK, C_FV, C_FF = (i * GROUP for i in range(9))
C_NQ = C_FF + FOX_HEADS
C_NKV = C_NQ + GROUP
C_NG = C_NKV + 6 * HD
N_IN2 = C_NG + 3 * NSA_HEADS

VA = {"b_ada": 0, "g_mix": 48, "c": 56}
VA_ROWS = 64
VB = {"g_ffn": 0, "g_final": 8, "norm_mix_2": 16, "norm_ffn_2": 24, "out_norm_2": 32, "g_q_lora": 40,
      "g_kv_lora": 46, "lru_conv_b_2": 48, "lru_b_gates_2": 50, "lru_lambda_2": 54,
      "lru_conv_w_2": 56, "sc_conv_w_2": 64, "fox_q": 70, "fox_k": 71, "nsa_q": 72, "nsa_kskw": 73,
      "nsa_kc": 74, "pos": 75}
VB_ROWS = 75 + 32

ARENA = 12780
RAW = 6
HL = 6
AHEAD = 4
PW = 1024
ADA = 6 * KC
ADA_FIRST, ADA_UP = 2 * KC, 5 * KC
ADA_JOB = [range(ADA_FIRST + 3 * c // 2, ADA_FIRST + 3 * (c + 1) // 2) for c in range(16)]
MAGIC = 1.5 * 2.0 ** 23
C1 = 6.28125
C2 = float(np.float32(np.round((2 * math.pi - C1) * 2 ** 21) / 2 ** 21))
C3 = 2 * math.pi - C1 - C2


def shape_constants():
    def buckets(far):
        d = np.arange(SEQ)
        log = 16 + (np.log(np.maximum(d, 1).astype(np.float32) / np.float32(16))
                    / np.float32(math.log(far / 16)) * np.float32(16)).astype(np.int32)
        return np.where(d < 16, d, np.minimum(log, BUCKETS - 1))
    onehot = np.zeros((BUCKETS + 1, 2, FW), np.float32)
    dist = np.arange(SEQ)
    seen = (dist <= 128).astype(int) + (dist % 4 == 0) + (dist % 16 == 0)
    add = [np.where(seen > 0, 8 * np.log(np.maximum(seen, 1)), NEG), np.zeros(SEQ)]
    for n, far in enumerate((2048, 128)):
        onehot[BUCKETS, n, :] = NEG
        at = SEQ - 1 - dist
        onehot[buckets(far), n, at] = 8.0
        onehot[BUCKETS, n, at] = add[n]
    p, j = np.arange(P)[:, None], np.arange(P)[None, :]
    diag = np.where(j <= p, 0.0, NEG)
    mask = np.concatenate([diag, np.zeros((P, P)), diag], 1).astype(np.float32)
    half = np.kron(np.eye(2), np.ones((HD, HD))).astype(np.float32)
    freq = np.float32(10000.0) ** (-np.arange(HALF, dtype=np.float32) / np.float32(HALF))
    sel = np.zeros((FOX_HEADS, FOX_HEADS, P), np.float32)
    sel[np.arange(FOX_HEADS), np.arange(FOX_HEADS)] = 1.0
    return {"k_ident": np.eye(P, dtype=np.float32), "k_half": half, "k_onehot": onehot,
            "k_mask": mask, "k_freq": np.broadcast_to(freq, (P, HALF)).astype(np.float32).copy(),
            "k_sel": sel}


def build(nc, I, out):
    f32, f32r, i32 = mybir.dt.float32, mybir.dt.float32r, mybir.dt.int32
    ALU, ACT = mybir.AluOpType, mybir.ActivationFunctionType
    mult, add, sub = ALU.mult, ALU.add, ALU.subtract
    ds = bass.ds

    def cols(w, c, n, k0=0, kn=KC):
        return w[k0 * P:(k0 + kn) * P, c:c + n].rearrange("(k p) n -> p k n", p=P)

    w_in, w_in2 = I["w_in"], I["w_in_2"]
    splits, directs = [], []

    def panel(name, parts):
        splits.append((name, parts))

    def chunk(name, w, c, n=P):
        panel(name, [(0, KC, n, 0, n, cols(w, c, n))])

    def ada(m, behind):
        directs.append((behind, [(0, 1, D, 0, D, cols(I["w_ada"], m // KC * D, D, m % KC, 1))]))

    for m in range(ADA_FIRST):
        ada(m, -1)
    for c in range(6):
        chunk("cq", w_in, C_CQ + c * P)
    for c in range(2):
        chunk("ckv", w_in, C_KV + c * P)
    chunk("kr", w_in, C_KR, ROPE)
    for c in range(4):
        chunk("aq", w_in, c * P)
    for c in range(4):
        chunk("ak", w_in, AW + c * P)
    for k in range(4):
        panel("av", [(0, 2, AW, 0, AW, cols(w_in, 2 * AW, AW, 2 * k, 2))])
    for k in range(6):
        panel("uq", [(0, 1, 768, 0, 768, cols(I["w_uq"], 0, 768, k, 1))])
    for k in range(2):
        panel("ukv", [(0, 1, 1024, 0, 1024, cols(I["w_ukv"], 0, 1024, k, 1))])
    for c in range(16):
        chunk("gate", w_in, C_GA + c * P)
        for m in ADA_JOB[c]:
            ada(m, len(splits) - 1 + AHEAD)
    for c in range(KC):
        panel("up", [(0, 4, P, 0, P, cols(I["w_up_a"], c * P, P, 0, 4)),
                     (512, 4, P, 0, P, cols(I["w_up_b"], c * P, P, 0, 4))])
        ada(ADA_UP + c, len(splits) - 1 + AHEAD)
    for c in range(KC):
        chunk("wo", I["w_o"], c * P)

    def ffn_panels(f):
        splits.extend([("ffn%d" % f, None)] * (3 * FC))

    ffn_panels(0)
    for c in range(2):
        chunk("fq", w_in2, C_FQ + c * P)
    for c in range(2):
        chunk("fk", w_in2, C_FK + c * P)
    for c in range(2):
        chunk("nq", w_in2, C_NQ + c * P)
    chunk("kcvc", w_in2, C_NKV)
    panel("kskw", [(0, KC, P, 0, HD, cols(w_in2, C_NKV + 2 * HD, HD)),
                   (0, KC, P, HD, HD, cols(w_in2, C_NKV + 4 * HD, HD))])
    panel("fg", [(0, KC, 16, 0, FOX_HEADS, cols(w_in2, C_FF, FOX_HEADS)),
                 (0, KC, 16, FOX_HEADS, 12, cols(w_in2, C_NG, 12))])
    panel("vsvw", [(0, KC, P, 0, HD, cols(w_in2, C_NKV + 3 * HD, HD)),
                   (0, KC, P, HD, HD, cols(w_in2, C_NKV + 5 * HD, HD))])
    for k in range(2):
        panel("fv", [(0, 4, GROUP, 0, GROUP, cols(w_in2, C_FV, GROUP, 4 * k, 4))])
    FILL = [C_LX, C_LX + P, C_SC, C_SC + P, C_SX, C_SX + P, C_SB, C_SB + P, C_LG, C_LG + P]
    for c in FILL[:4]:
        chunk("fill", w_in2, c)
    for kv in range(2):
        for half in range(2):
            directs.append((len(splits) - 1 + AHEAD,
                            [(0, 8, P, 0, P, I["nsa_cmp_w1_2"][kv].rearrange("(k p) n -> p k n", p=P)
                              [:, 8 * half:8 * half + 8, :])]))
    for c in FILL[4:]:
        chunk("fill", w_in2, c)
    for c in range(KC):
        chunk("wout", I["w_out_2"], c * P)
    ffn_panels(1)
    panels, at = [], {}
    for n in range(-1, len(splits)):
        if n >= 0:
            at.setdefault(splits[n][0], len(panels))
            panels.append((True, splits[n][1]))
        panels += [(False, parts) for behind, parts in directs if behind == n]
    NPANEL = len(panels)
    order, count = [], [0, 0]
    for split, _ in panels:
        order.append(count[split])
        count[split] += 1

    def nth(name, k=0):
        return order[at[name]] + k

    ctx = ExitStack()
    with ctx:
        def sb(name, shape, dt=f32):
            return ctx.enter_context(nc.sbuf_tensor(name, shape, dt))

        def sem(name):
            return ctx.enter_context(nc.semaphore(name))

        raw = sb("raw", [P, RAW, PW])
        w_hi = sb("w_hi", [P, HL, PW], f32r)
        w_lo = sb("w_lo", [P, HL, PW], f32r)
        xT = sb("xT", [P, KC, SEQ])
        sq = sb("sq", [P, KC, SEQ])
        rms = sb("rms", [P, SEQ])
        inv = sb("inv", [P, SEQ])
        h_hi = sb("h_hi", [P, KC, SEQ], f32r)
        h_lo = sb("h_lo", [P, KC, SEQ], f32r)
        mix_hi = sb("mix_hi", [P, KC, SEQ], f32r)
        mix_lo = sb("mix_lo", [P, KC, SEQ], f32r)
        bias = sb("bias", [P, NB, FW])
        zb = sb("zb", [P, 2, FW])
        zc = sb("zc", [P, 2, 2, 16])
        ptb = sb("ptb", [P, 2, FW])
        qkb = sb("qkb", [MQ, 4, P])
        g_hi = sb("g_hi", [P, 2, SEQ], f32r)
        g_lo = sb("g_lo", [P, 2, SEQ], f32r)
        ident = sb("ident", [P, P])
        half1 = sb("half1", [P, P])
        ones = sb("ones", [P, SEQ])
        mask = sb("mask", [P, FW])
        va = sb("va", [P, VA_ROWS])
        vb = sb("vb", [P, VB_ROWS])
        mod = sb("mod", [P, 6, KC])
        gs = sb("gs", [P, 2, KC])
        cond = sb("cond", [P, KC])
        small = sb("small", [P, 160])
        arena = sb("arena", [P, ARENA])

        where = [0]

        def take(*shape, rows=P, start=None):
            if start is not None:
                where[0] = start
            n = int(np.prod(shape))
            v = arena[0:rows, where[0]:where[0] + n]
            where[0] += n
            assert where[0] <= ARENA, where
            names = "abcd"[:len(shape)]
            if len(shape) > 1:
                v = v.rearrange("p (%s) -> p %s" % (" ".join(names), " ".join(names)),
                                **dict(zip(names[1:], shape[1:])))
            return v

        aqT, akT = take(4, SEQ, start=0), take(4, SEQ)
        a_v = take(TT, AW)
        q_tm, k_tm = take(TT, MH, MQ), take(TT, MH, MQ)
        m_v = take(TT, MH * MV)
        kr = take(TT, 1, ROPE)
        rt = [take(TT, MH, HALF) for _ in range(4)]
        gates = take(16, SEQ)
        x_tm = take(TT, D, start=0)
        va_rows = take(P, rows=VA_ROWS)
        vb_rows = take(P, rows=VB_ROWS)
        onehot = take(2, FW, rows=BUCKETS + 1)
        rel = take(NB, P, rows=BUCKETS + 1)
        relc = take(NB, rows=BUCKETS + 1)
        ang, turns, arg = (take(TT, HALF) for _ in range(3))
        acc01 = take(2, D)
        frow = take(NB, FW, start=ARENA - NB * FW)
        sg, hf = take(2, SEQ, start=0), take(2, SEQ)
        fqT, fkT = take(2, SEQ), take(2, SEQ)
        f_v = take(TT, GROUP)
        nqT = take(2, SEQ)
        kcvc, kcvc_x, kskw, kskw_x = (take(SEQ) for _ in range(4))
        n_v = take(TT, 2, HD)
        fg = take(TT, 16)
        gate2 = take(TT, 12)
        gb_row = take(12)
        xb = take(2, 16, NCMP)
        crow = take(FOX_HEADS, SEQ)
        dec = take(FOX_HEADS, FW)
        cf = take(3, SEQ, rows=FOX_HEADS)
        selb = take(FOX_HEADS, P, rows=FOX_HEADS)
        fbias = take(1, rows=FOX_HEADS)
        hid = take(2, 16)
        kcT = take(16)
        kcq = take(16)
        v_c = take(HD, rows=16)
        w2k = take(2, HD)
        w2v = take(HD)
        lx = take(2, SEQ + 3)
        lg, s_b, s_c = take(2, SEQ), take(2, SEQ), take(2, SEQ)
        sx = take(2, SEQ + 2)
        lw = take(2, 2, P)
        free = bias[:, 0:A_HEADS, :].rearrange("p a b -> p (a b)")
        yT = free[:, 0:KC * SEQ].rearrange("p (a b) -> p a b", b=SEQ)
        xc = free[:, 8 * SEQ:10 * SEQ].rearrange("p (a b) -> p a b", b=SEQ)
        ra = free[:, 10 * SEQ:12 * SEQ].rearrange("p (a b) -> p a b", b=SEQ)
        ia = crow[:, 0:2, :]

        def col(c, n=1, rows=P):
            return small[0:rows, c:c + n]
        eps_c, hpi_c = col(0), col(1)
        pos_f = col(4, 2)
        invq, invkv = col(6, 2), col(8, 2)
        nm, den, rec = small[:, 12:16], small[:, 16:20], small[:, 20:24]
        mx = small[:, 24:28]
        ccol = small[:, 28:36]
        spt = [small[:, 40 + 2 * i:42 + 2 * i] for i in range(8)]
        pos_i = sb("pos_i", [P, 2], i32)
        freq = sb("freq", [P, HALF])
        cosT, sinT = sb("cosT", [P, TT, HALF]), sb("sinT", [P, TT, HALF])

        ps = [ctx.enter_context(nc.psum_tensor(f"ps{i}", [P, 512], f32)) for i in range(8)]
        LIN = [ps[4], ps[5]]
        MOD = ps[6][:, 0:48]
        NRM = ps[7][:, 0:SEQ]
        frow_dram = nc.dram_tensor("head_rows", [P, NB * FW], f32, kind="Internal").ap()

        raw_in = [sem(f"raw_in{i}") for i in range(RAW)]
        hi_done, lo_done, panel_used = sem("hi_done"), sem("lo_done"), sem("panel_used")
        ada_used, cmp_used = sem("ada_used"), sem("cmp_used")
        S = {}

        def s(name):
            if name not in S:
                S[name] = sem(name)
            return S[name]

        class Line:

            def __init__(self, eng, name):
                self.eng, self.own, self.n = eng, s(name), {}
                self.last = None

            def __call__(self, ins, name=None):
                sm = self.own if name is None else s(name)
                ins.then_inc(sm, 1)
                self.n[name] = self.n.get(name, 0) + 1
                self.last = (sm, self.n[name])

            def settle(self):
                self.eng.wait_ge(*self.last)

            def skip(self, name, k):
                self.n[name] = self.n.get(name, 0) + k

        loads = {
            "in_x": [(x_tm, I["x"].rearrange("(t p) d -> p t d", p=P))],
            "in_va": [(va_rows[0:48, :], I["b_ada"].rearrange("(r p) -> r p", p=P)),
                      (va_rows[48:56, :], I["g_mix"].rearrange("(r p) -> r p", p=P)),
                      (va_rows[56:64, :], I["c"].rearrange("(r p) -> r p", p=P))],
            "in_id": [(ident[:, :], I["k_ident"])],
            "in_rel": [(onehot, I["k_onehot"]),
                       (relc[0:BUCKETS, 0:A_HEADS], I["rel_bias"].rearrange("h b -> b h")),
                       (relc[0:BUCKETS, A_HEADS:NB], I["rel_bias_2"])],
            "in_pos": [(pos_i[:, :], I["positions"].rearrange("(t p) -> p t", p=P)),
                       (freq[:, :], I["k_freq"])],
            "in_mask": [(mask[:, :], I["k_mask"]), (half1[:, :], I["k_half"])],
        }

        def vrow(name, rows=None):
            r = VB[name]
            src = I[name]
            return (vb_rows[r:r + src.shape[0] // P, :], src.rearrange("(r p) -> r p", p=P))
        loads["in_vb"] = [vrow(n) for n in ("g_ffn", "g_final", "norm_mix_2", "norm_ffn_2", "out_norm_2",
                                            "g_q_lora", "g_kv_lora", "lru_conv_b_2", "lru_b_gates_2",
                                            "lru_lambda_2", "lru_conv_w_2", "sc_conv_w_2")]
        fqk, nqk = I["fox_qk_norm_2"], I["nsa_qk_norm_2"]
        for n, (a, b) in {"fox_q": (fqk[0:1], fqk[0:1]), "fox_k": (fqk[1:2], fqk[1:2]),
                          "nsa_q": (nqk[0:1], nqk[0:1]), "nsa_kskw": (nqk[2:3], nqk[3:4]),
                          "nsa_kc": (nqk[1:2], nqk[1:2])}.items():
            for x, y in enumerate((a, b)):
                loads["in_vb"].append((vb_rows[VB[n]:VB[n] + 1, x * HD:(x + 1) * HD], y))
        loads["in_vb"].append((vb_rows[VB["pos"]:VB["pos"] + 32, :],
                               I["nsa_cmp_pos_2"].rearrange("(r p) -> r p", p=P)))
        loads2 = {
            "in_b2": [(selb, I["k_sel"]), (fbias, I["fox_f_bias_2"]),
                      (gb_row, I["nsa_gate_bias_2"].partition_broadcast(P)),
                      (w2k[:, 0, :], I["nsa_cmp_w2_2"][0]), (w2k[:, 1, :], I["nsa_cmp_w2_2"][0]),
                      (w2v, I["nsa_cmp_w2_2"][1])],
            "in_lw": [(lw[64 * (h % 2):64 * (h % 2) + 64, g, h // 2, 64 * (h % 2):64 * (h % 2) + 64],
                       I["lru_w_gates_2"][g, h]) for g in range(2) for h in range(4)],
        }

        def arrived(eng, name):
            eng.wait_ge(s(name), 16 * len((loads | loads2)[name]))

        JOBS = [("A", h) for h in range(A_HEADS)] + [("M", h) for h in range(MH)]
        JOBS2 = [("F", h) for h in range(FOX_HEADS)]
        for h in range(NSA_HEADS):
            JOBS2 += [("S", h), ("W", h), ("C", h)]
        N1, N2 = len(JOBS), len(JOBS2)
        ADA_SUM = {next(c for c in range(N1) if KC * (g + 1) - 1 in ADA_JOB[c]) + 1: g for g in (2, 3, 4)}
        ALL = JOBS + JOBS2
        OUT = []
        for k, h in ALL:
            OUT.append((OUT[-1] + (k not in "WC")) if OUT else 0)
        closes = [g + 1 == len(ALL) or OUT[g + 1] != OUT[g] for g in range(len(ALL))]
        outputs, freed = [], []
        lin_freed = [0, 0]

        def output(name, k=0, free=None):
            b = len(outputs) % 2
            if free is None:
                lin_freed[b] += 1
                free = ("lin_free%d" % b, lin_freed[b])
            outputs.append(nth(name, k))
            freed.append(free)
            return len(outputs) - 1

        L = {}
        for name, n in (("cq", 6), ("ckv", 2), ("kr", 1), ("aq", 4), ("ak", 4)):
            L[name] = [output(name, c) for c in range(n)]
        L["av"] = [output("av", 3) for _ in range(TT)]
        L["gate"] = [output("gate", c) for c in range(16)]
        L["up"] = [output("up", c) for c in range(KC)]
        L["wo"] = [output("wo", c, ("x_ready", c + 1)) for c in range(KC)]
        L["ffn0"] = [output("ffn0", 0 if j == 0 else 3 * j - 1, ("hf_done", j + 1)) for j in range(FC)]
        for name, n in (("fq", 2), ("fk", 2), ("nq", 2), ("kcvc", 1), ("kskw", 1), ("fg", 1), ("vsvw", 1)):
            L[name] = [output(name, c) for c in range(n)]
        L["fv"] = [output("fv", 1) for _ in range(TT)]
        L["fill"] = [output("fill", c) for c in range(len(FILL))]
        L["wout"] = [output("wout", c, ("x_ready", 24 + c + 1)) for c in range(KC)]
        L["ffn1"] = [output("ffn1", 0 if j == 0 else 3 * j - 1, ("hf_done", FC + j + 1)) for j in range(FC)]

        def lin(l, n=SEQ, a=0):
            return LIN[l % 2][:, a:a + n]

        def bank_of(f, j):
            return LIN[(L["ffn%d" % f][0] + j) % 2]

        def await_out(eng, l):
            eng.wait_ge(panel_used, outputs[l] + 1)

        def free_name(l):
            return "lin_free%d" % (l % 2)

        def vcol(name, c=0, n=1):
            return vb[:, VB[name] + c:VB[name] + c + n]

        QK2 = [("fq", 0, fqT[:, 0, :], "fox_q"), ("fq", 1, fqT[:, 1, :], "fox_q"),
               ("fk", 0, fkT[:, 0, :], "fox_k"), ("fk", 1, fkT[:, 1, :], "fox_k"),
               ("nq", 0, nqT[:, 0, :], "nsa_q"), ("nq", 1, nqT[:, 1, :], "nsa_q"),
               ("kskw", 0, kskw, "nsa_kskw")]
        FILL_TO = [lx[:, 0, 3:], lx[:, 1, 3:], s_c[:, 0, :], s_c[:, 1, :], sx[:, 0, 2:], sx[:, 1, 2:],
                   s_b[:, 0, :], s_b[:, 1, :], lg[:, 0, :], lg[:, 1, :]]
        EARLY = 4

        def o_region(o):
            r = HD * (o % 2)
            return ps[7][r:r + HD, SEQ * ((o // 2) % 2):SEQ * ((o // 2) % 2) + SEQ]

        def o_rows(buf, o):
            r = HD * (o % 2)
            return buf[r:r + HD, o // 2, :]

        def ada_acc(g):
            if g < 2:
                return acc01[:, g, :]
            return {2: sq[:, 0:4, :], 3: sq[:, 4:8, :], 4: sq[:, 0:4, :], 5: aqT}[g].rearrange("p a b -> p (a b)")

        closers = [g for g in range(len(ALL)) if closes[g]]

        def z_parts(g):
            if ALL[g][0] == "C":
                return [zc[:, g % 2, 0, 0:NCMP0], zc[:, g % 2, 1, 0:NCMP]]
            return [zb[:, g % 2, 0:P], zb[:, g % 2, P:FW]]

        def pair(buf, g):
            return buf[:, 2 * (g % 2):2 * (g % 2) + 2]

        def hi_lo(m, a, n):
            return w_hi[:, m % HL, a:a + n], w_lo[:, m % HL, a:a + n]

        def f_pos(what, j):
            if what == "d":
                return 3 * j + 4 if j < FC - 1 else 3 * FC - 1
            return (0 if j == 0 else 3 * j - 1) + (what == "u")

        def f_src(f, what, j):
            w = ("w_gate", "w_up", "w_down") if f == 0 else ("w_gate_up_2", "w_gate_up_2", "w_down_2")
            if what == "d":
                return 1, D, I[w[2]][ds(j * P, P), :].rearrange("(k p) n -> p k n", p=P)
            base = D_FF if (f == 1 and what == "u") else 0
            src = I[w["gu".index(what)]][:, ds(j * P + base, P)]
            return KC, P, src.rearrange("(k p) n -> p k n", p=P)

        raw_count, raised = [], [0] * RAW
        for n, (_, parts) in enumerate(panels):
            raised[n % RAW] += 16 * (len(parts) if parts else 1)
            raw_count.append(raised[n % RAW])
        index_of = [n for n in range(NPANEL) if panels[n][0]]
        direct_of = [n for n in range(NPANEL) if not panels[n][0]]
        widths = [max(a + kn * c for a, kn, c, _, _, _ in panels[n][1]) if panels[n][1] else PW
                  for n in index_of]
        NS = len(index_of)
        ITER = (FC - 4) // 2
        assert RAW == 6 and HL == 6

        ctx.enter_context(nc.allow_non_contiguous_dma(reason="a few small vectors laid out by partition"))
        block = ctx.enter_context(nc.Block())

        @block.sync
        def _(sp):
            def load(n, parts, i=0):
                if n >= RAW:
                    o = n - RAW
                    if panels[o][0]:
                        sp.wait_ge(lo_done, order[o] + 1 + i * 6)
                    else:
                        sp.wait_ge(*((ada_used, order[o] + 1) if order[o] < ADA else (cmp_used, order[o] + 1 - ADA)))
                for a, kn, c, off, w, src in parts:
                    dst = raw[:, n % RAW, a:a + kn * c].rearrange("p (k n) -> p k n", n=c)[:, :, off:off + w]
                    sp.dma_start(dst, src).then_inc(raw_in[n % RAW], 16)

            def ffn(f):
                n0 = at["ffn%d" % f]

                def one(n, what, j, i=0):
                    kn, c, src = f_src(f, what, j)
                    load(n, [(0, kn, c, 0, c, src)], i)
                one(n0, "g", 0)
                one(n0 + 1, "u", 0)
                for j in (1, 2):
                    one(n0 + f_pos("g", j), "g", j)
                    one(n0 + f_pos("u", j), "u", j)
                    one(n0 + f_pos("d", j - 1), "d", j - 1)
                with sp.Fori(0, ITER) as i:
                    for j in (3, 4):
                        one(n0 + f_pos("g", j), "g", i * 2 + j, i)
                        one(n0 + f_pos("u", j), "u", i * 2 + j, i)
                        one(n0 + f_pos("d", j - 1), "d", i * 2 + (j - 1), i)
                e = n0 + 3 * FC - 4
                one(e, "g", FC - 1)
                one(e + 1, "u", FC - 1)
                one(e + 2, "d", FC - 2)
                one(e + 3, "d", FC - 1)

            n = 0
            while n < NPANEL:
                if panels[n][1] is None:
                    ffn(int(n != at["ffn0"]))
                    n += 3 * FC
                else:
                    load(n, panels[n][1])
                    n += 1
            for t in range(TT):
                sp.wait_ge(s("y_copied"), 2 * (t + 1))
                sp.dma_start(out[t * P:(t + 1) * P, :], arena[:, t * D:(t + 1) * D]).then_inc(s("out_done"), 16)
            sp.wait_ge(s("out_done"), 16 * TT)

        class Splitter:

            def __init__(self, part):
                self.part, self.next = part, 0

            def ahead(self, m):
                while self.next < min(m + 1 + AHEAD, NS):
                    self.part(self.next, 0)
                    self.next += 1

        @block.scalar
        def _(act):
            A = nc.scalar.activation
            line = Line(act, "act_step")

            def split_hi(m, i):
                n = index_of[m]
                act.wait_ge(raw_in[n % RAW], raw_count[n] + i * 16)
                if m >= HL:
                    act.wait_ge(panel_used, m - HL + 1 + i * 6)
                w = widths[m]
                A(w_hi[:, m % HL, 0:w], raw[:, n % RAW, 0:w], ACT.Copy).then_inc(hi_done, 1)
            split = Splitter(split_hi)

            for name in ("in_id", "in_va", "in_x", "in_rel", "in_pos", "in_mask", "in_vb"):
                for dst, src in loads[name]:
                    act.dma_start(dst, src).then_inc(s(name), 16)
            act.wait_ge(s("va_t"), 1)
            line(A(va[:, :], ps[5][:, 0:VA_ROWS], ACT.Copy), "va_ready")
            line.settle()
            line(A(cond[:, :], va[:, 56:64], ACT.Silu), "cond_ready")
            for b in range(4):
                act.wait_ge(s("x_t"), b + 1)
                line(A(xT[:, 2 * b:2 * b + 2, :].rearrange("p a b -> p (a b)"), ps[b][:, :], ACT.Copy), "x_copied")
            line.settle()

            def square(c, base=None):
                if base is not None:
                    act.wait_ge(s("x_ready"), base + c + 1)
                line(A(sq[:, c, :], xT[:, c, :], ACT.Square), "sq_ready")

            def root(k):
                act.wait_ge(s("ss_done"), k + 1)
                if k:
                    act.wait_ge(s("inv_ready"), k)
                line(A(rms[:, :], NRM, ACT.Sqrt, scale=1.0 / D, bias=eps_c), "rms_ready")

            def highs(k, shift=None):
                for c in range(KC):
                    act.wait_ge(s("h_ready"), 8 * k + c + 1)
                    if shift is None:
                        line(A(h_hi[:, c, :], sq[:, c, :], ACT.Copy), "h_hi")
                    else:
                        line(A(h_hi[:, c, :], sq[:, c, :], ACT.Identity, bias=mod[:, shift, c:c + 1]), "h_hi")

            for c in range(KC):
                square(c)
            act.wait_ge(s("const_ready"), 1)
            root(0)
            act.wait_ge(s("vb_t"), 1)
            line(A(vb[:, :], ps[4][:, 0:VB_ROWS], ACT.Copy), "vb_ready")
            for h in range(NB):
                act.wait_ge(s("frow_mm"), h + 1)
                line(A(frow[:, h, :], ps[h % 4][:, 0:FW], ACT.Copy), "frow_copied")
            act.wait_ge(s("arg_ready"), 1)
            line(A(sinT[:, :, :], ang, ACT.Sin))
            line(A(cosT[:, :, :], arg, ACT.Sin, scale=-1.0, bias=hpi_c), "trig_ready")
            split.ahead(-1)
            highs(0, shift=0)

            act.wait_ge(s("h_lo"), 8)
            for c in range(8):
                l = (L["cq"] + L["ckv"])[c]
                split.ahead(outputs[l])
                await_out(act, l)
                line(A(sq[:, c, :], lin(l), ACT.Square), "lat_sq")
                line(A(mix_hi[:, c, :], lin(l), ACT.Copy, scale=vcol("g_q_lora", c)), "lat_hi")
                if c == 1:
                    act.wait_ge(s("frow_copied"), NB)
                    act.dma_start(frow_dram, frow.rearrange("p a b -> p (a b)")).then_inc(s("frow_out"), 16)
            l = L["kr"][0]
            split.ahead(outputs[l])
            await_out(act, l)
            line(A(kr.rearrange("p t a r -> p (t a r)"), lin(l, TT * ROPE), ACT.Copy), free_name(l))
            for c, l in enumerate(L["aq"] + L["ak"]):
                split.ahead(outputs[l])
                await_out(act, l)
                line(A((aqT if c < 4 else akT)[:, c % 4, :], lin(l), ACT.Copy), free_name(l))
                if c == 2:
                    act.wait_ge(s("frow_out"), 16)
                    for a, n, off in ((P, SEQ, P - 1), (0, P, SEQ - 1)):
                        act.dma_start(bias[:, :, a:a + n],
                                      bass.AP(frow_dram.tensor, off, [[NB * FW - 1, P], [FW, NB], [1, n]]))\
                            .then_inc(s("bias_in"), 16)
            split.ahead(nth("av", 3))
            for t, l in enumerate(L["av"]):
                await_out(act, l)
                line(A(a_v[:, t, :], lin(l, 512), ACT.Copy), free_name(l))
            act.wait_ge(s("lat_ss"), 1)
            for q, n in enumerate((Q_LORA, KV_LORA)):
                line(A(small[:, 56 + 2 * q:58 + 2 * q], ps[7][:, 2 * q:2 * q + 2], ACT.Sqrt, scale=1.0 / n,
                       bias=eps_c), "lat_rms")
            split.ahead(nth("uq", 5))
            act.wait_ge(s("lat_inv"), 1)
            act.wait_ge(panel_used, nth("uq", 5) + 1)
            for b in range(4):
                t, q = b // 2, b % 2
                line(A(q_tm[:, t, 4 * q:4 * q + 4, :].rearrange("p a b -> p (a b)"), ps[b][:, 0:384], ACT.Copy,
                       scale=invq[:, t:t + 1]), "q_copied")
            split.ahead(nth("ukv", 1))
            act.wait_ge(panel_used, nth("ukv", 1) + 1)
            for b in range(4):
                t, q = b // 2, b % 2
                v = ps[b][:, :].rearrange("p (h c) -> p h c", c=NOPE + MV)
                line(A(m_v[:, t, 256 * q:256 * q + 256].rearrange("p (h c) -> p h c", c=MV), v[:, :, NOPE:], ACT.Copy,
                       scale=invkv[:, t:t + 1]), "v_copied")

            def exps(g):
                act.wait_ge(s("z_ready"), g + 1)
                for t, z in enumerate(z_parts(g)):
                    line(A(z, z, ACT.Exp, bias=pair(nm, g)[:, t:t + 1], accum_out=pair(den, g)[:, t:t + 1]), "e_ready")

            def pt_copy(g):
                act.wait_ge(s("pt_done"), g + 1)
                if g >= 2:
                    act.wait_ge(s("pv_done"), g - 1)
                if ALL[g][0] == "C":
                    line(A(ptb[0:NCMP, g % 2, 0:SEQ], ps[2][0:NCMP, 0:SEQ], ACT.Copy), "pt_copied")
                else:
                    line(A(ptb[:, g % 2, :], ps[2][:, 0:FW], ACT.Copy), "pt_copied")

            def o_copy(g):
                if closes[g]:
                    act.wait_ge(s("pv_done"), g + 1)
                    o = OUT[g]
                    if g < N1:
                        line(A(o_rows(mix_hi, o), o_region(o), ACT.Copy), "o_hi")
                    else:
                        line(A(o_rows(yT, 8 + o - 16), o_region(o), ACT.Copy), "o_hi")

            def qk_copy(h):
                act.wait_ge(s("qkt_done"), h + 1)
                if h >= 1:
                    act.wait_ge(s("s_done"), A_HEADS + h)
                line(A(qkb[:, :, :].rearrange("p a b -> p (a b)"), ps[3][0:MQ, :], ACT.Copy), "qk_copied")

            act.wait_ge(s("lam_abs"), 1)
            line(A(spt[0], spt[5], ACT.Exp, scale=-1.0), "lam_exp")
            for g in range(N1 + 2):
                if g < N1:
                    split.ahead(nth("gate", g))
                    exps(g)
                if A_HEADS <= g + 1 < N1:
                    qk_copy(g + 1 - A_HEADS)
                if g < N1:
                    l = L["gate"][g]
                    await_out(act, l)
                    line(A(gates[:, g, :], lin(l), ACT.Copy), free_name(l))
                if 1 <= g <= N1:
                    pt_copy(g - 1)
                if g >= 2:
                    o_copy(g - 2)
            split.ahead(nth("up", 0))
            for c in range(KC):
                for k in (c, 8 + c):
                    line(A(gates[:, k, :], gates[:, k, :], ACT.Sigmoid), "sig_done")
            for c in range(KC):
                split.ahead(nth("up", c))
                act.wait_ge(s("merged"), c + 1)
                line(A(h_hi[:, c, :], sq[:, c, :], ACT.Copy), "m_hi")
            for c in range(KC):
                split.ahead(nth("wo", c))
                act.wait_ge(s("m_lo"), 8)
                square(c, 0)
            root(1)
            highs(1, shift=3)

            def ffn(f):
                m0 = nth("ffn%d" % f)
                assert split.next == m0 + AHEAD, (split.next, m0)

                def hidden(j, i, more):
                    J = FC * f + j
                    for m in more[:1]:
                        split_hi(m, i)
                    act.wait_ge(panel_used, m0 + f_pos("u", j) + 1 + i * 6)
                    line(A(sg[:, j % 2, :], bank_of(f, j)[:, 0:SEQ], ACT.Silu), "silu_done")
                    for m in more[1:2]:
                        split_hi(m, i)
                    act.wait_ge(s("hf_done"), J + 1 + i * 2)
                    if j >= 2:
                        act.wait_ge(panel_used, m0 + f_pos("d", j - 2) + 1 + i * 6)
                    line(A(g_hi[:, j % 2, :], hf[:, j % 2, :], ACT.Copy), "g_hi")
                    for m in more[2:]:
                        split_hi(m, i)
                e = split.next
                hidden(0, 0, [e, e + 1])
                for j in (1, 2):
                    hidden(j, 0, [e + 3 * j - 1 + k for k in range(3)])
                with act.Fori(0, ITER) as i:
                    for j in (3, 4):
                        hidden(j, i, [e + 3 * j - 1 + k for k in range(3)])
                line.skip("silu_done", 2 * (ITER - 1))
                line.skip("g_hi", 2 * (ITER - 1))
                split.next = e + 3 * FC - 4
                more = [m for m in range(split.next, split.next + 3) if m < NS]
                hidden(FC - 1, 0, more)
                split.next += len(more)
            ffn(0)
            for c in range(KC):
                square(c, 8)
            root(2)
            act.wait_ge(s("inv_ready"), 3)
            for c in range(KC):
                square(c, 16)
            root(3)
            highs(2)

            act.wait_ge(s("h_lo"), 24)
            for q, (name, c, dst, _) in enumerate(QK2[:6]):
                l = L[name][c]
                split.ahead(outputs[l])
                await_out(act, l)
                line(A(sq[:, q, :], lin(l), ACT.Square), "qk_sq")
                line(A(dst, lin(l), ACT.Copy), free_name(l))
            l = L["kcvc"][0]
            split.ahead(outputs[l])
            await_out(act, l)
            line(A(kcvc, lin(l), ACT.Copy), free_name(l))
            l = L["kskw"][0]
            split.ahead(outputs[l])
            await_out(act, l)
            line(A(sq[:, 6, :], lin(l), ACT.Square), "qk_sq")
            line(A(kskw, lin(l), ACT.Copy), free_name(l))
            l = L["fg"][0]
            split.ahead(outputs[l])
            await_out(act, l)
            line(A(fg.rearrange("p t a -> p (t a)"), lin(l, TT * 16), ACT.Copy), free_name(l))
            l = L["vsvw"][0]
            split.ahead(outputs[l])
            await_out(act, l)
            line(A(n_v.rearrange("p t a b -> p (t a b)"), lin(l, TT * P), ACT.Copy), free_name(l))
            split.ahead(nth("fv", 1))
            for t, l in enumerate(L["fv"]):
                await_out(act, l)
                line(A(f_v[:, t, :], lin(l, GROUP), ACT.Copy), free_name(l))
            for b in range(4):
                n = 2 if b < 3 else 1
                act.wait_ge(s("qk_ss"), 2 * b + n)
                line(A(sq[:, 2 * b:2 * b + n, :].rearrange("p a b -> p (a b)"), ps[b][:, 0:n * SEQ], ACT.Sqrt,
                       scale=1.0 / HD, bias=eps_c), "qk_rms")
            for q in range(EARLY):
                l = L["fill"][q]
                split.ahead(outputs[l])
                await_out(act, l)
                line(A(FILL_TO[q], lin(l), ACT.Copy), free_name(l))
            act.wait_ge(s("f_abs"), 1)
            line(A(cf[:, 1, :], cf[:, 1, :], ACT.Exp, scale=-1.0))
            line.settle()
            line(A(cf[:, 1, :], cf[:, 1, :], ACT.Ln, bias=ones[0:FOX_HEADS, 0:1]), "f_log")
            act.wait_ge(s("gate_sum"), 1)
            line(A(gate2, gate2, ACT.Sigmoid), "gate2_ready")
            for q in range(4):
                act.wait_ge(s("lru_mm"), 2 * (q // 2) + 2)
                line(A((ra, ia)[q // 2][:, q % 2, :], ps[q // 2][:, SEQ * (q % 2):SEQ * (q % 2) + SEQ], ACT.Sigmoid,
                       bias=vcol("lru_b_gates_2", q)), "lru_sig")
            act.wait_ge(cmp_used, 4)
            line(A(hid[:, :, 0:NCMP], ps[7][:, 0:32].rearrange("p (a b) -> p a b", b=16)[:, :, 0:NCMP],
                   ACT.Gelu_apprx_tanh), "hid_ready")
            act.wait_ge(s("kc_mm"), 1)
            line(A(kcT[:, 0:NCMP], ps[7][:, 32:32 + NCMP], ACT.Copy))
            line(A(kcq[:, 0:NCMP], ps[7][:, 32:32 + NCMP], ACT.Square), "kc_sq")
            act.wait_ge(s("vc_mm"), 1)
            line(A(v_c[0:NCMP, :], ps[6][0:NCMP, 64:64 + HD], ACT.Copy), "vc_ready")
            act.wait_ge(s("kc_ss"), 1)
            line(A(kcq[:, 0:NCMP], ps[7][:, 48:48 + NCMP], ACT.Sqrt, scale=1.0 / HD, bias=eps_c), "kc_rms")

            for g in range(N1, N1 + N2 + 2):
                q = EARLY + g - N1
                if g < N1 + N2:
                    if q < len(FILL):
                        split.ahead(nth("fill", q))
                    exps(g)
                    if q < len(FILL):
                        l = L["fill"][q]
                        await_out(act, l)
                        line(A(FILL_TO[q], lin(l), ACT.Copy), free_name(l))
                if N1 < g <= N1 + N2:
                    pt_copy(g - 1)
                if g >= N1 + 2:
                    o_copy(g - 2)
            act.wait_ge(s("lru_c"), 1)
            for c in range(2):
                line(A(yT[:, c, :], ra[:, c, :], ACT.Tanh, scale=spt[7][:, c:c + 1]), "lru_tanh")
                line(A(ra[:, c, :], ra[:, c, :], ACT.Exp, scale=spt[6][:, c:c + 1]), "lru_a")
            line(A(lg, lg, ACT.Gelu_apprx_tanh), "lg_ready")
            act.wait_ge(s("lru_w"), 1)
            line(A(yT[:, 0:2, :], yT[:, 0:2, :], ACT.Sqrt), "lru_sqrt")
            for k, c in enumerate((2, 3, 4, 5, 6, 7, 0, 1)):
                if c in (2, 3):
                    act.wait_ge(s("yb_ready"), 1)
                if c < 2:
                    act.wait_ge(s("ya_ready"), 1)
                if c == 4:
                    act.wait_ge(s("o_hi"), 24)
                line(A(sq[:, c, :], yT[:, c, :], ACT.Square), "y_sq")
            for b in range(2):
                act.wait_ge(s("y_ss"), 4)
                line(A(arena[:, b * 512:(b + 1) * 512], ps[b][:, :], ACT.Sqrt, scale=1.0 / GROUP, bias=eps_c), "y_rms")
            for c in range(KC):
                act.wait_ge(s("y_ready"), c + 1)
                line(A(mix_hi[:, c, :], yT[:, c, :], ACT.Copy), "y_hi")
            for c in range(KC):
                split.ahead(nth("wout", c))
                if c == 0:
                    act.wait_ge(s("y_lo"), 8)
                square(c, 24)
            root(4)
            highs(3)
            ffn(1)
            for b in range(4):
                act.wait_ge(s("y_t"), b + 1)
                line(A(arena[:, b * 512:(b + 1) * 512], ps[b][:, :], ACT.Copy), "y_copied")

        @block.vector
        def _(dve):
            V = nc.vector
            line = Line(dve, "dve_step")
            stt = V.scalar_tensor_tensor

            def split_lo(m, i):
                n, w = index_of[m], widths[m]
                dve.wait_ge(hi_done, m + 1 + i * 6)
                V.tensor_tensor(w_lo[:, m % HL, 0:w], raw[:, n % RAW, 0:w], w_hi[:, m % HL, 0:w].bitcast(f32),
                                sub).then_inc(lo_done, 1)
            split = Splitter(split_lo)

            line(V.memset(ones[:, :], 1.0))
            line(V.memset(eps_c, EPS))
            line(V.memset(hpi_c, math.pi / 2))
            line(V.memset(zc[:, :, :, :], 0.0), "const_ready")
            line(V.memset(rel[BUCKETS:BUCKETS + 1], 1.0))
            arrived(dve, "in_rel")
            line(V.tensor_copy(rel[0:BUCKETS], relc[0:BUCKETS, :].unsqueeze(2).to_broadcast([BUCKETS, NB, P])), "rel_ready")
            arrived(dve, "in_pos")
            line(V.tensor_copy(pos_f, pos_i[:, :]))
            line.settle()
            for t in range(TT):
                line(V.tensor_scalar(ang[:, t, :], freq[:, :], pos_f[:, t:t + 1], None, mult))
            line.settle()
            line(V.tensor_scalar(turns, ang, 1.0 / (2 * math.pi), MAGIC, mult, add))
            line.settle()
            line(V.tensor_scalar(turns, turns, MAGIC, None, sub))
            for c in (C1, C2, C3):
                line.settle()
                line(stt(out=ang, in0=turns, scalar=-c, in1=ang, op0=mult, op1=add))
            line.settle()
            line(V.tensor_scalar(ang, ang, 3.1415925, -3.1415925, ALU.min, ALU.max))
            line.settle()
            line(stt(out=arg, in0=ang, scalar=-1.0, in1=ang, op0=mult, op1=ALU.max), "arg_ready")

            def inverse(k):
                dve.wait_ge(s("rms_ready"), k + 1)
                line(V.reciprocal(inv[:, :], rms[:, :]), "inv_ready")

            def modulate(g, n=1):
                dve.wait_ge(s("mod_sum"), g + n)
                line(V.tensor_tensor(mod[:, g:g + n, :].rearrange("p a b -> p (a b)"), MOD[:, 8 * g:8 * (g + n)],
                                     va[:, 8 * g:8 * (g + n)], add))
                line.settle()

            def ada(m):
                n, g, k = direct_of[m], m // KC, m % KC
                acc, w = ada_acc(g), raw[:, direct_of[m] % RAW, :]
                dve.wait_ge(raw_in[n % RAW], raw_count[n])
                if k == 0:
                    ins = V.tensor_scalar(acc, w, cond[:, k:k + 1], None, mult)
                else:
                    dve.wait_ge(ada_used, m)
                    ins = stt(out=acc, in0=w, scalar=cond[:, k:k + 1], in1=acc, op0=mult, op1=add)
                ins.then_inc(ada_used, 1)

            dve.wait_ge(s("cond_ready"), 1)
            for m in range(KC):
                ada(m)
            inverse(0)
            for m in range(KC, 2 * KC):
                ada(m)
            split.ahead(-AHEAD)
            modulate(0, 2)
            line(stt(out=gs[:, 0, :], in0=mod[:, 1, :], scalar=1.0, in1=va[:, 48:56], op0=add, op1=mult))

            def normed(k, gain, shift=None):
                def low(c):
                    dve.wait_ge(s("h_hi"), 8 * k + c + 1)
                    hi = h_hi[:, c, :].bitcast(f32)
                    if shift is None:
                        line(V.tensor_tensor(h_lo[:, c, :], sq[:, c, :], hi, sub), "h_lo")
                    else:
                        line(stt(out=h_lo[:, c, :], in0=sq[:, c, :], scalar=mod[:, shift, c:c + 1], in1=hi,
                                 op0=add, op1=sub), "h_lo")
                for c in range(KC):
                    line(stt(out=sq[:, c, :], in0=xT[:, c, :], scalar=gain[:, c:c + 1], in1=inv[:, :], op0=mult,
                             op1=mult), "h_ready")
                    if c >= 2:
                        low(c - 2)
                low(KC - 2)
                low(KC - 1)
            dve.wait_ge(s("x_copied"), 4)
            line.settle()
            normed(0, gs[:, 0, :], 0)
            split.ahead(-1)

            dve.wait_ge(s("vb_ready"), 1)
            lam = vcol("lru_lambda_2", 0, 2)
            line(stt(out=spt[5], in0=lam, scalar=-1.0, in1=lam, op0=mult, op1=ALU.max), "lam_abs")
            for c, l in enumerate(L["cq"] + L["ckv"]):
                split.ahead(outputs[l])
                dve.wait_ge(s("lat_hi"), c + 1)
                line(stt(out=mix_lo[:, c, :], in0=lin(l), scalar=vcol("g_q_lora", c), in1=mix_hi[:, c, :].bitcast(f32),
                         op0=mult, op1=sub), free_name(l))
            split.ahead(nth("av", 3))
            dve.wait_ge(s("lat_rms"), 2)
            line(V.reciprocal(small[:, 6:10], small[:, 56:60]), "lat_inv")
            split.ahead(nth("ukv", 1))
            dve.wait_ge(panel_used, nth("ukv", 1) + 1)
            for b in range(4):
                t, q = b // 2, b % 2
                dve.wait_ge(s("v_copied"), b + 1)
                v = ps[b][:, :].rearrange("p (h c) -> p h c", c=NOPE + MV)
                line(V.tensor_scalar(k_tm[:, t, 4 * q:4 * q + 4, 0:NOPE], v[:, :, 0:NOPE], invkv[:, t:t + 1], None, mult),
                     "k_copied")

            arrived(dve, "in_mask")
            dve.wait_ge(s("bias_in"), 32)

            def scores(g):
                kind, h = ALL[g]
                dve.wait_ge(s("s_done"), g + 1)
                if g >= 2:
                    dve.wait_ge(s("pt_done"), g - 1)
                if kind == "C":
                    b = bias[:, A_HEADS + h, :]
                    src = [ps[g % 2][:, 0:NCMP0], ps[g % 2][:, P:P + NCMP]]
                    near = CMP_LEN - 1
                    ins = [b[:, SEQ + near:FW:CMP_STRIDE], b[:, P + near:FW:CMP_STRIDE]]
                else:
                    b = {"A": bias[:, h, :], "M": mask[:, :], "F": dec[:, h % FOX_HEADS, :]}.get(
                        kind, bias[:, A_HEADS + h % NSA_HEADS, :])
                    src = [ps[g % 2][:, 0:P], ps[g % 2][:, P:FW]]
                    ins = [b[:, 0:P], b[:, P:FW]]
                for t, z in enumerate(z_parts(g)):
                    line(V.tensor_tensor_reduce(out=z, in0=src[t], in1=ins[t], scale=M_SCALE if kind == "M" else SCALE,
                                                scalar=-3e38, op0=add, op1=ALU.max, accum_out=pair(mx, g)[:, t:t + 1]))
                line.settle()
                line(V.tensor_scalar(pair(nm, g), pair(mx, g), -1.0, None, mult), "z_ready")

            def probabilities(g):
                kind, h = ALL[g]
                dve.wait_ge(s("e_ready"), 2 * (g + 1))
                line(V.reciprocal(pair(rec, g), pair(den, g)))
                line.settle()
                if kind == "C":
                    line(V.tensor_scalar(pair(mx, g), pair(mx, g), NEG / 100, None, ALU.is_gt))
                    line.settle()
                    line(V.tensor_tensor(pair(rec, g), pair(rec, g), pair(mx, g), mult))
                    line.settle()
                if kind in "SWC":
                    b = 4 * "CSW".index(kind) + h
                    line(V.tensor_tensor(pair(rec, g), pair(rec, g), gate2[:, :, b:b + 1].rearrange("p t a -> p (t a)"), mult))
                    line.settle()
                for t, z in enumerate(z_parts(g)):
                    line(V.tensor_scalar(z, z, pair(rec, g)[:, t:t + 1], None, mult), "p_ready")

            for g in range(N1 + 2):
                if g < N1:
                    scores(g)
                    split.ahead(nth("gate", g))
                    probabilities(g)
                    for m in ADA_JOB[g]:
                        if m == 4 * KC:
                            dve.wait_ge(s("mod_sum"), 3)
                        ada(m)
                if g >= 2:
                    o = OUT[g - 2]
                    dve.wait_ge(s("o_hi"), o + 1)
                    line(V.tensor_tensor(o_rows(mix_lo, o), o_region(o), o_rows(mix_hi, o).bitcast(f32), sub), "o_lo")
            modulate(2, 3)
            line(stt(out=gs[:, 1, :], in0=mod[:, 4, :], scalar=1.0, in1=vb[:, 0:8], op0=add, op1=mult))
            split.ahead(nth("up", 0))
            for c, l in enumerate(L["up"]):
                split.ahead(outputs[l])
                await_out(dve, l)
                dve.wait_ge(s("sig_done"), 2 * c + 2)
                line(V.tensor_tensor(gates[:, c, :], lin(l), gates[:, c, :], mult))
                line(V.tensor_tensor(gates[:, 8 + c, :], lin(l, SEQ, SEQ), gates[:, 8 + c, :], mult), free_name(l))
                ada(ADA_UP + c)
            modulate(5)
            for c, l in enumerate(L["wo"]):
                split.ahead(outputs[l])
                await_out(dve, l)
                line(stt(out=xT[:, c, :], in0=lin(l), scalar=mod[:, 2, c:c + 1], in1=xT[:, c, :], op0=mult, op1=add),
                     "x_ready")
            inverse(1)
            line.settle()
            normed(1, gs[:, 1, :], 3)

            def ffn(f):
                m0 = nth("ffn%d" % f)

                def hidden(j, i, more):
                    J = FC * f + j
                    for m in more[:1]:
                        split_lo(m, i)
                    dve.wait_ge(s("silu_done"), J + 1 + i * 2)
                    line(V.tensor_tensor(hf[:, j % 2, :], sg[:, j % 2, :], bank_of(f, j)[:, SEQ:512], mult), "hf_done")
                    for m in more[1:2]:
                        split_lo(m, i)
                    dve.wait_ge(s("g_hi"), J + 1 + i * 2)
                    line(V.tensor_tensor(g_lo[:, j % 2, :], hf[:, j % 2, :], g_hi[:, j % 2, :].bitcast(f32), sub), "g_lo")
                    for m in more[2:]:
                        split_lo(m, i)
                assert split.next == m0 + AHEAD
                e = split.next
                hidden(0, 0, [e, e + 1])
                for j in (1, 2):
                    hidden(j, 0, [e + 3 * j - 1 + k for k in range(3)])
                with dve.Fori(0, ITER) as i:
                    for j in (3, 4):
                        hidden(j, i, [e + 3 * j - 1 + k for k in range(3)])
                line.skip("hf_done", 2 * (ITER - 1))
                line.skip("g_lo", 2 * (ITER - 1))
                split.next = e + 3 * FC - 4
                more = [m for m in range(split.next, split.next + 3) if m < NS]
                hidden(FC - 1, 0, more)
                split.next += len(more)
                dve.wait_ge(panel_used, m0 + 3 * FC)
                for c in range(KC):
                    acc = ps[c // 2][:, SEQ * (c % 2):SEQ * (c % 2) + SEQ]
                    if f == 0:
                        line(stt(out=xT[:, c, :], in0=acc, scalar=mod[:, 5, c:c + 1], in1=xT[:, c, :], op0=mult,
                                 op1=add), "x_ready")
                    else:
                        line(V.tensor_tensor(xT[:, c, :], acc, xT[:, c, :], add), "x_ready")
            ffn(0)
            inverse(2)
            line.settle()
            for c in range(KC):
                line(stt(out=xT[:, c, :], in0=xT[:, c, :], scalar=vcol("g_final", c), in1=inv[:, :], op0=mult,
                         op1=mult), "x_ready")
            inverse(3)
            line.settle()
            normed(2, vcol("norm_mix_2", 0, 8))

            split.ahead(nth("fq", 0))
            dve.wait_ge(s("lam_exp"), 1)
            e_, s_, s2, acc_, t_ = spt[0], spt[1], spt[2], spt[3], spt[4]
            line(V.tensor_scalar(t_, e_, 2.0, None, add))
            line.settle()
            line(V.reciprocal(t_, t_))
            line.settle()
            line(V.tensor_tensor(s_, e_, t_, mult))
            line.settle()
            line(V.tensor_tensor(s2, s_, s_, mult))
            line(V.memset(acc_, 1.0 / 15))
            for k in (13, 11, 9, 7, 5, 3, 1):
                line.settle()
                line(V.tensor_tensor(acc_, acc_, s2, mult))
                line.settle()
                line(V.tensor_scalar(acc_, acc_, 1.0 / k, None, add))
            line.settle()
            line(stt(out=acc_, in0=acc_, scalar=2.0, in1=s_, op0=mult, op1=mult))
            line.settle()
            line(V.tensor_scalar(t_, vcol("lru_lambda_2", 0, 2), -1.0, 0.0, mult, ALU.max))
            line.settle()
            line(V.tensor_tensor(acc_, acc_, t_, add))
            line.settle()
            line(V.tensor_scalar(spt[7], acc_, 8.0, None, mult))
            line(V.tensor_scalar(spt[6], acc_, -8.0, None, mult), "lru_c")
            for name in ("kskw", "fg", "vsvw"):
                split.ahead(nth(name))
            split.ahead(nth("fv", 1))
            for b in range(4):
                n = 2 if b < 3 else 1
                dve.wait_ge(s("qk_rms"), b + 1)
                v = sq[:, 2 * b:2 * b + n, :].rearrange("p a b -> p (a b)")
                line(V.reciprocal(v, v))
                line.settle()
                for q in range(2 * b, 2 * b + n):
                    _, _, dst, gain = QK2[q]
                    line(stt(out=dst, in0=dst, scalar=vcol(gain), in1=sq[:, q, :], op0=mult, op1=mult), "qk_ready")
            split.ahead(nth("fill", 0))
            arrived(dve, "in_b2")
            dve.wait_ge(s("f_t"), 1)
            line(V.tensor_scalar(cf[:, 0, :], ps[6][0:FOX_HEADS, 0:SEQ], fbias, None, add))
            line.settle()
            line(stt(out=cf[:, 1, :], in0=cf[:, 0, :], scalar=-1.0, in1=cf[:, 0, :], op0=mult, op1=ALU.max), "f_abs")
            line(V.tensor_scalar(cf[:, 0, :], cf[:, 0, :], 0.0, None, ALU.min))
            line(V.tensor_tensor(gate2, fg[:, :, 4:16], gb_row.unsqueeze(1).to_broadcast([P, TT, 12]), add), "gate_sum")
            split.ahead(nth("fill", 1))

            dve.wait_ge(s("pads"), 1)

            def conv(dst, src, taps, name, first, c, tell=None):
                for k in range(taps):
                    tap = vcol(name, 2 * k + c)
                    x = src[:, c, k:k + SEQ]
                    if k == 0:
                        line(V.tensor_scalar(dst, x, tap, None, mult) if first is None
                             else V.tensor_scalar(dst, x, tap, first, mult, add))
                    else:
                        line(stt(out=dst, in0=x, scalar=tap, in1=dst, op0=mult, op1=add),
                             tell if k == taps - 1 else None)
                    line.settle()
            for c in range(2):
                l = L["fill"][c]
                dve.wait_ge(s(free_name(l)), freed[l][1])
                conv(xc[:, c, :], lx, 4, "lru_conv_w_2", vcol("lru_conv_b_2", c), c, "xc_ready")
            dve.wait_ge(s("f_log"), 1)
            line(V.tensor_tensor(cf[:, 1, :], cf[:, 1, :], cf[:, 0, :], sub))
            line.settle()
            line(V.tensor_tensor_scan(cf[:, 2, :], ones[0:FOX_HEADS, :], cf[:, 1, :], 0.0, mult, add))
            line.settle()
            line(V.tensor_scalar(cf[:, 2, :], cf[:, 2, :], 8.0, None, mult), "c_ready")
            dve.wait_ge(s("ccol_mm"), 1)
            line(V.tensor_copy(ccol, ps[6][:, 304:312]))
            line.settle()
            for h in range(FOX_HEADS):
                dve.wait_ge(s("crow_mm"), 2 * (h // 2) + 2)
                row = ps[2 + h // 2][:, SEQ * (h % 2):SEQ * (h % 2) + SEQ]
                line(stt(out=dec[:, h, 0:P], in0=row[:, 0:P], scalar=ccol[:, h:h + 1], in1=mask[:, 0:P],
                         op0=sub, op1=add))
                line(stt(out=dec[:, h, P:FW], in0=row, scalar=ccol[:, 4 + h:5 + h], in1=mask[:, P:FW],
                         op0=sub, op1=add), "dec_ready")
            split.ahead(nth("fill", 3))
            dve.wait_ge(s("kc_rms"), 1)
            line(V.reciprocal(kcq[:, 0:NCMP], kcq[:, 0:NCMP]))
            line.settle()
            line(stt(out=kcT[:, 0:NCMP], in0=kcT[:, 0:NCMP], scalar=vcol("nsa_kc"), in1=kcq[:, 0:NCMP], op0=mult,
                     op1=mult), "kc_ready")

            dve.wait_ge(s("gate2_ready"), 1)
            for g in range(N1, N1 + N2):
                q = EARLY + g - N1
                scores(g)
                if q < len(FILL):
                    split.ahead(nth("fill", q))
                probabilities(g)
                if g == N1 + 7:
                    for c in range(2):
                        l = L["fill"][6 + c]
                        dve.wait_ge(s(free_name(l)), freed[l][1])
                    for c in range(2):
                        line(V.tensor_tensor(sx[:, c, 2:], sx[:, c, 2:], s_c[:, c, :], mult))
                        line.settle()
                        conv(s_c[:, c, :], sx, 3, "sc_conv_w_2", None, c)
                        line(V.tensor_tensor(yT[:, 2 + c, :], s_b[:, c, :], s_c[:, c, :], mult),
                             None if c == 0 else "yb_ready")
                if g == N1 + 9:
                    dve.wait_ge(s("lru_sig"), 4)
                    line(V.tensor_tensor(ia, ia, xc, mult))
            dve.wait_ge(s("lru_tanh"), 2)
            line(V.tensor_scalar(xc, yT[:, 0:2, :], 1.0, None, add))
            line.settle()
            line(V.reciprocal(xc, xc))
            line.settle()
            line(stt(out=yT[:, 0:2, :], in0=yT[:, 0:2, :], scalar=2.0, in1=xc, op0=mult, op1=mult), "lru_w")
            dve.wait_ge(s("lru_sqrt"), 1)
            line(V.tensor_tensor(ia, ia, yT[:, 0:2, :], mult))
            line.settle()
            for c in range(2):
                line(V.tensor_tensor_scan(xc[:, c, :], ra[:, c, :], ia[:, c, :], 0.0, mult, add))
            line.settle()
            dve.wait_ge(s("lg_ready"), 1)
            line(V.tensor_tensor(yT[:, 0:2, :], xc, lg, mult), "ya_ready")
            split.ahead(nth("wout", 0) - 1)
            for b in range(2):
                dve.wait_ge(s("y_rms"), b + 1)
                v = arena[:, b * 512:(b + 1) * 512]
                line(V.reciprocal(v, v))
                line.settle()
                for c in range(4 * b, 4 * b + 4):
                    g = c // 2
                    line(stt(out=yT[:, c, :], in0=yT[:, c, :], scalar=vcol("out_norm_2", c),
                             in1=arena[:, g * SEQ:(g + 1) * SEQ], op0=mult, op1=mult), "y_ready")
            for c in range(KC):
                dve.wait_ge(s("y_hi"), c + 1)
                line(V.tensor_tensor(mix_lo[:, c, :], yT[:, c, :], mix_hi[:, c, :].bitcast(f32), sub), "y_lo")
            for c, l in enumerate(L["wout"]):
                split.ahead(outputs[l])
                await_out(dve, l)
                line(V.tensor_tensor(xT[:, c, :], lin(l), xT[:, c, :], add), "x_ready")
            inverse(4)
            line.settle()
            normed(3, vcol("norm_ffn_2", 0, 8))
            ffn(1)

        @block.gpsimd
        def _(pool):
            G = nc.gpsimd
            line = Line(pool, "pool_step")

            def rotate(x, h, tell=None):
                a, b = x[:, :, :, 0:HALF], x[:, :, :, HALF:ROPE]
                t = [r[:, :, 0:h, :] for r in rt]
                co = cosT[:, :, :].unsqueeze(2).to_broadcast([P, TT, h, HALF])
                si = sinT[:, :, :].unsqueeze(2).to_broadcast([P, TT, h, HALF])
                for dst, x_, y_ in ((t[0], a, co), (t[1], b, si), (t[2], a, si), (t[3], b, co)):
                    line(G.tensor_tensor(dst, x_, y_, mult))
                line.settle()
                line(G.tensor_tensor(a, t[0], t[1], sub))
                line(G.tensor_tensor(b, t[2], t[3], add), tell)
                line.settle()
            pool.wait_ge(s("trig_ready"), 1)
            l = L["kr"][0]
            pool.wait_ge(s(free_name(l)), freed[l][1])
            rotate(kr, 1)
            line(G.tensor_copy(k_tm[:, :, :, NOPE:MQ], kr.to_broadcast([P, TT, MH, ROPE])), "rope_k")
            pool.wait_ge(s("q_copied"), 4)
            rotate(q_tm[:, :, :, NOPE:MQ], MH, "rope_q")
            for c, l in enumerate(L["up"]):
                pool.wait_ge(s(free_name(l)), freed[l][1])
                line(G.tensor_tensor(sq[:, c, :], gates[:, c, :], gates[:, 8 + c, :], add), "merged")
                pool.wait_ge(s("m_hi"), c + 1)
                line(G.tensor_tensor(h_lo[:, c, :], sq[:, c, :], h_hi[:, c, :].bitcast(f32), sub), "m_lo")
            pool.wait_ge(s("x_ready"), 24)
            line(G.memset(lw, 0.0))
            line(G.memset(lx[:, :, 0:3], 0.0))
            line(G.memset(sx[:, :, 0:2], 0.0), "pads")
            line.settle()
            for name, group in loads2.items():
                for dst, src in group:
                    pool.dma_start(dst, src).then_inc(s(name), 16)
            l = L["kcvc"][0]
            pool.wait_ge(s(free_name(l)), freed[l][1])
            for a in (0, HD):
                pool.dma_start(kcvc_x[a:a + HD, :], kcvc[HD - a:2 * HD - a, :]).then_inc(s("kcvc_x_in"), 16)
            pool.wait_ge(s("kcvc_x_in"), 32)
            for kv, lower, upper in ((0, kcvc, kcvc_x), (1, kcvc_x, kcvc)):
                for e, x in ((0, lower), (1, upper)):
                    r = slice(HD * e, HD * e + HD)
                    x16 = x[r, :].rearrange("p (n s) -> p s n", s=CMP_STRIDE)
                    for n in range(CMP_LEN // CMP_STRIDE):
                        k0 = VB["pos"] + 16 * kv + 8 * n
                        pos = vb[r, k0:k0 + 8].unsqueeze(2).to_broadcast([HD, 8, NCMP])
                        last = kv == 1 and e == 1 and n == 1
                        line(G.tensor_tensor(xb[r, kv, 8 * n:8 * n + 8, :], x16[:, e:CMP_STRIDE:2, n:n + NCMP], pos, add),
                             "xb_ready" if last else None)
            pool.wait_ge(s("qk_ready"), 7)
            for a in (0, HD):
                pool.dma_start(kskw_x[a:a + HD, :], kskw[HD - a:2 * HD - a, :]).then_inc(s("kskw_x_in"), 16)

        @block.tensor
        def _(pe):
            T = nc.tensor
            line = Line(pe, "pe_step")
            used = [0]

            def take_panel(m, last_of):
                last_of.then_inc(panel_used, 1)

            def product(dst, stat, mov, start, stop, shared=False):
                kw = {"skip_group_check": True} if shared else {}
                T.matmul(dst, stat[0], mov[0], start=start, stop=False, **kw)
                T.matmul(dst, stat[0], mov[1], start=False, stop=False, **kw)
                return T.matmul(dst, stat[1], mov[0], start=False, stop=stop, **kw)

            def hx(c):
                return h_hi[:, c, :], h_lo[:, c, :]

            def mxp(c):
                return mix_hi[:, c, :], mix_lo[:, c, :]

            def await_split(m, i=0):
                pe.wait_ge(lo_done, m + 1 + i * 6)

            def await_bank(l):
                if l >= 2:
                    name, v = freed[l - 2]
                    pe.wait_ge(s(name), v)

            def chunk_out(l, act, fresh=None):
                m = outputs[l]
                await_split(m)
                await_bank(l)
                for k in range(KC):
                    if fresh is not None:
                        pe.wait_ge(s(fresh[0]), fresh[1] + k + 1)
                    ins = product(lin(l), hi_lo(m, k * P, P), act(k), k == 0, k == KC - 1)
                ins.then_inc(panel_used, 1)

            def tokens_out(ls, ms, kn, n):
                for l in ls:
                    await_bank(l)
                for x, m in enumerate(ms):
                    await_split(m)
                    for k in range(kn):
                        a = hx(x * kn + k)
                        for t, l in enumerate(ls):
                            ins = product(lin(l, n), [v[:, t * P:(t + 1) * P] for v in a], hi_lo(m, k * n, n),
                                          x == 0 and k == 0, x == len(ms) - 1 and k == kn - 1)
                    ins.then_inc(panel_used, 1)

            def ada_sum(g):
                pe.wait_ge(ada_used, KC * (g + 1))
                for c in range(KC):
                    ins = T.matmul(MOD[:, KC * g + c:KC * g + c + 1], ada_acc(g)[:, c * P:(c + 1) * P], ones[:, 0:1],
                                   start=True, stop=True)
                line(ins, "mod_sum")

            arrived(pe, "in_id")
            arrived(pe, "in_va")
            line(T.transpose(ps[5][:, 0:VA_ROWS], va_rows, ident[0:VA_ROWS, 0:VA_ROWS]), "va_t")
            arrived(pe, "in_x")
            for b in range(4):
                for q in range(4):
                    c, t = 2 * b + q // 2, q % 2
                    ins = T.transpose(ps[b][:, q * P:(q + 1) * P], x_tm[:, t, c * P:(c + 1) * P], ident[:, :])
                line(ins, "x_t")
            arrived(pe, "in_vb")
            line(T.transpose(ps[4][:, 0:VB_ROWS], vb_rows[0:VB_ROWS], ident[0:VB_ROWS, 0:VB_ROWS]), "vb_t")

            def sums(k):
                for c in range(KC):
                    pe.wait_ge(s("sq_ready"), 8 * k + c + 1)
                    ins = T.matmul(NRM, ones[:, 0:P], sq[:, c, :], start=(c == 0), stop=(c == KC - 1))
                line(ins, "ss_done")
            pe.wait_ge(s("const_ready"), 1)
            sums(0)
            pe.wait_ge(s("rel_ready"), 1)
            pe.wait_ge(s("x_copied"), 4)
            for h in range(NB):
                if h >= 4:
                    pe.wait_ge(s("frow_copied"), h - 3)
                line(T.matmul(ps[h % 4][:, 0:FW], rel[:, h, :], onehot[:, int(h >= A_HEADS), :], start=True, stop=True),
                     "frow_mm")
            for g in range(2):
                ada_sum(g)

            for l in L["cq"] + L["ckv"]:
                chunk_out(l, hx, fresh=("h_lo", 0) if l == L["cq"][0] else None)
            m, l = nth("kr"), L["kr"][0]
            await_split(m)
            await_bank(l)
            for t in range(TT):
                for k in range(KC):
                    ins = product(lin(l, ROPE, ROPE * t), [v[:, t * P:(t + 1) * P] for v in hx(k)],
                                  hi_lo(m, k * ROPE, ROPE), k == 0, k == KC - 1)
            ins.then_inc(panel_used, 1)
            for l in L["aq"] + L["ak"]:
                chunk_out(l, hx)
            tokens_out(L["av"], [nth("av", k) for k in range(4)], 2, AW)
            pe.wait_ge(s("lat_sq"), 8)
            pe.wait_ge(s("vb_ready"), 1)
            for t in range(TT):
                for q, (c0, c1) in enumerate(((0, 6), (6, 8))):
                    for c in range(c0, c1):
                        ins = T.matmul(ps[7][:, 2 * q + t:2 * q + t + 1], sq[:, c, t * P:(t + 1) * P], ones[:, 0:1],
                                       start=(c == c0), stop=(c == c1 - 1))
            line(ins, "lat_ss")
            pe.wait_ge(s("frow_copied"), NB)
            for name, kn, n, c0 in (("uq", 6, 384, 0), ("ukv", 2, 512, 6)):
                for k in range(kn):
                    m = nth(name, k)
                    await_split(m)
                    if name == "ukv" and k == 0:
                        pe.wait_ge(s("q_copied"), 4)
                    for b in range(4):
                        t, q = b // 2, b % 2
                        ins = product(ps[b][:, 0:n], [v[:, t * P:(t + 1) * P] for v in mxp(c0 + k)],
                                      hi_lo(m, q * n, n), k == 0, k == kn - 1)
                    ins.then_inc(panel_used, 1)

            def qk_turn(h):
                if h >= 1:
                    pe.wait_ge(s("qk_copied"), h)
                for x, src in enumerate((q_tm, k_tm)):
                    for t in range(TT):
                        ins = T.transpose(ps[3][0:MQ, (2 * x + t) * P:(2 * x + t + 1) * P], src[:, t, h, :], ident[:, :])
                line(ins, "qkt_done")

            def make_scores(g):
                kind, h = ALL[g]
                if g >= 2:
                    pe.wait_ge(s("z_ready"), g - 1)
                r = slice(HD * (h % 2), HD * (h % 2) + HD)
                if kind == "A":
                    q, k = aqT[r, h // 2, :], akT[r, h // 2, :]
                elif kind == "M":
                    pe.wait_ge(s("qk_copied"), h + 1)
                    q, k = [qkb[:, 2 * x:2 * x + 2, :].rearrange("p a b -> p (a b)") for x in range(2)]
                elif kind == "F":
                    q, k = fqT[r, h // 2, :], fkT[r, h // 2, :]
                else:
                    q = nqT[r, h // 2, :]
                    own, other = kskw[r, :], kskw_x[r, :]
                    k = {"S": (own, other)[h % 2], "W": (other, own)[h % 2], "C": kcT[r, :]}[kind]
                if kind == "C":
                    T.matmul(ps[g % 2][:, 0:NCMP0], q[:, 0:P], k[:, 0:NCMP0], start=True, stop=True)
                    ins = T.matmul(ps[g % 2][:, P:P + NCMP], q[:, P:SEQ], k[:, 0:NCMP], start=True, stop=True)
                else:
                    T.matmul(ps[g % 2][:, 0:P], q[:, 0:P], k[:, 0:P], start=True, stop=True)
                    ins = T.matmul(ps[g % 2][:, P:FW], q[:, P:SEQ], k[:, 0:SEQ], start=True, stop=True)
                line(ins, "s_done")

            def turn(g):
                pe.wait_ge(s("p_ready"), 2 * (g + 1))
                if g >= 1:
                    pe.wait_ge(s("pt_copied"), g)
                if ALL[g][0] == "C":
                    for t in range(TT):
                        ins = T.transpose(ps[2][0:NCMP, t * P:(t + 1) * P], zc[:, g % 2, t, 0:NCMP], ident[:, :])
                else:
                    for b in range(3):
                        ins = T.transpose(ps[2][:, b * P:(b + 1) * P], zb[:, g % 2, b * P:(b + 1) * P], ident[:, :])
                line(ins, "pt_done")

            def gather(g):
                kind, h = ALL[g]
                o = OUT[g]
                pe.wait_ge(s("pt_copied"), g + 1)
                if o >= 2 and OUT[g - 1] != o:
                    pe.wait_ge(s("o_lo" if o - 2 < 16 else "o_hi"), o - 1)
                dst = o_region(o)
                first = kind in "AMFS"
                if kind == "C":
                    ins = T.matmul(dst, v_c[0:NCMP, :], ptb[0:NCMP, g % 2, 0:SEQ], start=False, stop=True,
                                   skip_group_check=True)
                else:
                    v = {"A": lambda t: a_v[:, t, HD * h:HD * h + HD], "M": lambda t: m_v[:, t, HD * h:HD * h + HD],
                         "F": lambda t: f_v[:, t, HD * h:HD * h + HD], "S": lambda t: n_v[:, t, 0, :],
                         "W": lambda t: n_v[:, t, 1, :]}[kind]
                    T.matmul(dst, v(0), ptb[:, g % 2, 0:SEQ], start=first, stop=False, skip_group_check=True)
                    ins = T.matmul(dst[:, P:SEQ], v(1), ptb[:, g % 2, SEQ:FW], start=False, stop=True,
                                   skip_group_check=True)
                line(ins, "pv_done")

            pe.wait_ge(s("v_copied"), 4)
            pe.wait_ge(s("k_copied"), 4)
            pe.wait_ge(s("bias_in"), 32)
            for g in range(N1 + 2):
                if g < N1:
                    make_scores(g)
                if g + 1 == A_HEADS:
                    pe.wait_ge(s("rope_q"), 1)
                if A_HEADS <= g + 1 < N1:
                    qk_turn(g + 1 - A_HEADS)
                if g < N1:
                    chunk_out(L["gate"][g], hx)
                if 1 <= g <= N1:
                    turn(g - 1)
                if g >= 2:
                    gather(g - 2)
                if g in ADA_SUM:
                    ada_sum(ADA_SUM[g])
            pe.wait_ge(s("o_lo"), 16)
            for c, l in enumerate(L["up"]):
                m = outputs[l]
                await_split(m)
                await_bank(l)
                for x in range(2):
                    for k in range(4):
                        ins = product(lin(l, SEQ, SEQ * x), hi_lo(m, (4 * x + k) * P, P), mxp(4 * x + k), k == 0, k == 3)
                ins.then_inc(panel_used, 1)
            ada_sum(5)
            for l in L["wo"]:
                chunk_out(l, hx, fresh=("m_lo", 0) if l == L["wo"][0] else None)
            sums(1)

            def ffn(f):
                m0 = nth("ffn%d" % f)
                def gate_up(j, i=0):
                    J = FC * f + j
                    if j >= 2:
                        pe.wait_ge(s("hf_done"), J - 1 + i * 2)
                    for x, what in enumerate("gu"):
                        m = m0 + f_pos(what, j)
                        await_split(m, i)
                        for k in range(KC):
                            if j == 0 and x == 0:
                                pe.wait_ge(s("h_lo"), 8 + 16 * f + k + 1)
                            ins = product(bank_of(f, j)[:, SEQ * x:SEQ * x + SEQ], hi_lo(m, k * P, P), hx(k), k == 0,
                                          k == KC - 1)
                        ins.then_inc(panel_used, 1)

                def down(j, i=0):
                    J = FC * f + j
                    m = m0 + f_pos("d", j)
                    await_split(m, i)
                    pe.wait_ge(s("g_lo"), J + 1 + i * 2)
                    for c in range(KC):
                        ins = product(ps[c // 2][:, SEQ * (c % 2):SEQ * (c % 2) + SEQ], hi_lo(m, c * P, P),
                                      (g_hi[:, j % 2, :], g_lo[:, j % 2, :]), j == 0 and c % 2 == 0, j == FC - 1,
                                      shared=True)
                    ins.then_inc(panel_used, 1)
                gate_up(0)
                for j in (1, 2):
                    gate_up(j)
                    down(j - 1)
                with pe.Fori(0, ITER) as i:
                    for j in (3, 4):
                        gate_up(j, i)
                        down(j - 1, i)
                gate_up(FC - 1)
                down(FC - 2)
                down(FC - 1)
            ffn(0)
            sums(2)
            sums(3)

            for l in L["fq"] + L["fk"] + L["nq"] + L["kcvc"] + L["kskw"]:
                chunk_out(l, hx, fresh=("h_lo", 16) if l == L["fq"][0] else None)
            for name, n in (("fg", 16), ("vsvw", P)):
                m, l = nth(name), L[name][0]
                await_split(m)
                await_bank(l)
                for t in range(TT):
                    for k in range(KC):
                        ins = product(lin(l, n, n * t), [v[:, t * P:(t + 1) * P] for v in hx(k)],
                                      hi_lo(m, k * n, n), k == 0, k == KC - 1)
                ins.then_inc(panel_used, 1)
            tokens_out(L["fv"], [nth("fv", k) for k in range(2)], 4, GROUP)
            arrived(pe, "in_mask")
            for q in range(7):
                pe.wait_ge(s("qk_sq"), q + 1)
                line(T.matmul(ps[q // 2][:, SEQ * (q % 2):SEQ * (q % 2) + SEQ], half1[:, :], sq[:, q, :],
                              start=True, stop=True), "qk_ss")
            l = L["fg"][0]
            pe.wait_ge(s(free_name(l)), freed[l][1])
            for t in range(TT):
                ins = T.transpose(ps[6][0:FOX_HEADS, t * P:(t + 1) * P], fg[:, t, 0:FOX_HEADS], ident[:, :])
            line(ins, "f_t")
            for l in L["fill"][:EARLY]:
                chunk_out(l, hx)
            pe.wait_ge(s("c_ready"), 1)
            arrived(pe, "in_b2")
            for t in range(TT):
                ins = T.matmul(ps[6][:, 304 + 4 * t:308 + 4 * t], cf[:, 2, t * P:(t + 1) * P], ident[0:FOX_HEADS, 0:FOX_HEADS],
                               start=True, stop=True)
            line(ins, "ccol_mm")
            for h in range(FOX_HEADS):
                line(T.matmul(ps[2 + h // 2][:, SEQ * (h % 2):SEQ * (h % 2) + SEQ], selb[:, h, :], cf[:, 2, :],
                              start=True, stop=True), "crow_mm")
            arrived(pe, "in_lw")
            pe.wait_ge(s("xc_ready"), 2)
            for q in range(4):
                g, c = q // 2, q % 2
                line(T.matmul(ps[g][:, SEQ * c:SEQ * c + SEQ], lw[:, g, c, :], xc[:, c, :], start=True, stop=True),
                     "lru_mm")
            pe.wait_ge(s("xb_ready"), 1)
            for kv in range(2):
                for half in range(2):
                    m = ADA + 2 * kv + half
                    n = direct_of[m]
                    pe.wait_ge(raw_in[n % RAW], raw_count[n])
                    for k in range(8):
                        last = T.matmul(ps[7][:, 16 * kv:16 * kv + NCMP], raw[:, n % RAW, k * P:(k + 1) * P],
                                        xb[:, kv, 8 * half + k, :], start=(half == 0 and k == 0),
                                        stop=(half == 1 and k == 7))
                    last.then_inc(cmp_used, 1)
            pe.wait_ge(s("hid_ready"), 1)
            pe.wait_ge(s("dec_ready"), 4)
            line(T.matmul(ps[7][:, 32:32 + NCMP], w2k.rearrange("p a b -> p (a b)"), hid[:, 0, 0:NCMP],
                          start=True, stop=True), "kc_mm")
            line(T.matmul(ps[6][0:NCMP, 64:64 + HD], hid[:, 1, 0:NCMP], w2v, start=True, stop=True), "vc_mm")
            pe.wait_ge(s("kc_sq"), 1)
            line(T.matmul(ps[7][:, 48:48 + NCMP], half1[:, :], kcq[:, 0:NCMP], start=True, stop=True), "kc_ss")
            pe.wait_ge(s("qk_ready"), 7)
            pe.wait_ge(s("lru_sig"), 4)
            pe.wait_ge(s("kc_ready"), 1)
            pe.wait_ge(s("vc_ready"), 1)
            for g in range(N1, N1 + N2 + 2):
                if g < N1 + N2:
                    if ALL[g] == ("S", 0):
                        pe.wait_ge(s("kskw_x_in"), 32)
                    make_scores(g)
                q = EARLY + g - N1
                if q < len(FILL):
                    chunk_out(L["fill"][q], hx)
                if N1 < g <= N1 + N2:
                    turn(g - 1)
                if g >= N1 + 2:
                    gather(g - 2)
            for n, grp in enumerate((1, 2, 3, 0)):
                pe.wait_ge(s("y_sq"), 2 * n + 2)
                for c in range(2):
                    ins = T.matmul(ps[grp // 2][:, SEQ * (grp % 2):SEQ * (grp % 2) + SEQ], ones[:, 0:P],
                                   sq[:, 2 * grp + c, :], start=(c == 0), stop=(c == 1))
                line(ins, "y_ss")
            for l in L["wout"]:
                chunk_out(l, mxp, fresh=("y_lo", 0) if l == L["wout"][0] else None)
            sums(4)
            ffn(1)
            for b in range(4):
                for q in range(4):
                    c = 4 * (b % 2) + q
                    pe.wait_ge(s("x_ready"), 32 + max(c + 1, 2 * b + 2))
                    ins = T.transpose(ps[b][:, q * P:(q + 1) * P], xT[:, c, (b // 2) * P:(b // 2 + 1) * P], ident[:, :])
                line(ins, "y_t")


INPUTS = {"x": (SEQ, D), "c": (D,), "positions": (SEQ,), "rel_bias": (A_HEADS, BUCKETS), "w_ada": (D, 6 * D),
          "b_ada": (6 * D,), "g_mix": (D,), "w_in": (D, -1), "g_q_lora": (Q_LORA,), "w_uq": (Q_LORA, MH * MQ),
          "g_kv_lora": (KV_LORA,), "w_ukv": (KV_LORA, MH * (NOPE + MV)), "w_up_a": (AW, D), "w_up_b": (MH * MV, D),
          "w_o": (D, D), "g_ffn": (D,), "w_gate": (D, D_FF), "w_up": (D, D_FF), "w_down": (D_FF, D), "g_final": (D,),
          "norm_mix_2": (D,), "w_in_2": (D, N_IN2), "lru_conv_w_2": (-1,), "lru_conv_b_2": (-1,),
          "lru_w_gates_2": (2, 4, HD, HD), "lru_b_gates_2": (-1,), "lru_lambda_2": (-1,), "sc_conv_w_2": (-1,),
          "fox_f_bias_2": (FOX_HEADS, 1), "fox_qk_norm_2": (2, HD), "nsa_qk_norm_2": (4, HD), "nsa_cmp_pos_2": (-1,),
          "nsa_cmp_w1_2": (2, CMP_LEN * HD, P), "nsa_cmp_w2_2": (2, P, HD), "nsa_gate_bias_2": (3 * NSA_HEADS,),
          "rel_bias_2": (BUCKETS, NSA_HEADS), "out_norm_2": (D,), "w_out_2": (D, D), "norm_ffn_2": (D,),
          "w_gate_up_2": (D, 2 * D_FF), "w_down_2": (D_FF, D)}


def kernel(**inputs):
    import concourse.bacc as bacc
    from concourse.bass_utils import run_bass_kernel_spmd

    nc = bacc.Bacc("TRN2", target_bir_lowering=False, num_devices=1)
    arrays = {name: np.ascontiguousarray(np.asarray(inputs[name]).reshape(shape)) for name, shape in INPUTS.items()}
    arrays.update(shape_constants())
    aps = {name: nc.dram_tensor(f"in_{name}", a.shape, mybir.dt.from_np(a.dtype), kind="ExternalInput").ap()
           for name, a in arrays.items()}
    out = nc.dram_tensor("out_x", (SEQ, D), mybir.dt.float32, kind="ExternalOutput").ap()
    build(nc, aps, out)
    ran = run_bass_kernel_spmd(nc, [{f"in_{name}": a for name, a in arrays.items()}], core_ids=[0])
    return ran.results[0]["out_x"].reshape(1, SEQ, D)
```

```python
import math
from contextlib import ExitStack

import numpy as np

import concourse.bass as bass
from concourse import mybir

P = 128
SEQ = 256
TT = SEQ // P
D = 1024
KC = D // P
A_HEADS, HD = 8, 64
AW = A_HEADS * HD
Q_LORA, KV_LORA, ROPE = 768, 256, 32
HALF = ROPE // 2
MH, NOPE, MV = 8, 64, 64
MQ = NOPE + ROPE
D_FF = -(-8 * D // (3 * 256)) * 256
FC = D_FF // P
GROUP = D // 4
FOX_HEADS = NSA_HEADS = GROUP // HD
CMP_LEN, CMP_STRIDE = 32, 16
NCMP = (SEQ - CMP_LEN) // CMP_STRIDE + 1
NCMP0 = (P - CMP_LEN) // CMP_STRIDE + 1
BUCKETS = 32
NEG = -1e30
EPS = 1e-6
SCALE = HD ** -0.5
M_SCALE = MQ ** -0.5
FW = 384
NB = A_HEADS + NSA_HEADS
NROW = 14

C_CQ = 3 * AW
C_KV = C_CQ + Q_LORA
C_KR = C_KV + KV_LORA
C_GA = C_KR + ROPE
C_GB = C_GA + D
C_LX, C_LG, C_SB, C_SC, C_SX, C_FQ, C_FK, C_FV, C_FF = (i * GROUP for i in range(9))
C_NQ = C_FF + FOX_HEADS
C_NKV = C_NQ + GROUP
C_NG = C_NKV + 6 * HD
N_IN2 = C_NG + 3 * NSA_HEADS

VA = {"b_ada": 0, "g_mix": 48, "c": 56}
VA_ROWS = 64
VB = {"g_ffn": 0, "g_final": 8, "norm_mix_2": 16, "norm_ffn_2": 24, "out_norm_2": 32, "g_q_lora": 40,
      "g_kv_lora": 46, "lru_conv_b_2": 48, "lru_b_gates_2": 50, "lru_lambda_2": 54,
      "lru_conv_w_2": 56, "sc_conv_w_2": 64, "fox_q": 70, "fox_k": 71, "nsa_q": 72, "nsa_kskw": 73,
      "nsa_kc": 74, "pos": 75}
VB_ROWS = 75 + 32

ARENA = 12780
RAW = 6
HL = 6
AHEAD = 4
PW = 1024
ADA = 6 * KC
ADA_FIRST, ADA_LAST = 2 * KC, 5 * KC
ADA_JOB = [range(ADA_FIRST + 3 * c // 2, ADA_FIRST + 3 * (c + 1) // 2) for c in range(16)]
MAGIC = 1.5 * 2.0 ** 23
C1 = 6.28125
C2 = float(np.float32(np.round((2 * math.pi - C1) * 2 ** 21) / 2 ** 21))
C3 = 2 * math.pi - C1 - C2


def shape_constants():
    def buckets(far):
        d = np.arange(SEQ)
        log = 16 + (np.log(np.maximum(d, 1).astype(np.float32) / np.float32(16))
                    / np.float32(math.log(far / 16)) * np.float32(16)).astype(np.int32)
        return np.where(d < 16, d, np.minimum(log, BUCKETS - 1))
    onehot = np.zeros((BUCKETS + 1, 2, FW), np.float32)
    dist = np.arange(SEQ)
    seen = (dist <= 128).astype(int) + (dist % 4 == 0) + (dist % 16 == 0)
    add = [np.where(seen > 0, 8 * np.log(np.maximum(seen, 1)), NEG), np.zeros(SEQ)]
    for n, far in enumerate((2048, 128)):
        onehot[BUCKETS, n, :] = NEG
        at = SEQ - 1 - dist
        onehot[buckets(far), n, at] = 8.0
        onehot[BUCKETS, n, at] = add[n]
    p, j = np.arange(P)[:, None], np.arange(P)[None, :]
    diag = np.where(j <= p, 0.0, NEG)
    mask = np.concatenate([diag, np.zeros((P, P)), diag], 1).astype(np.float32)
    half = np.kron(np.eye(2), np.ones((HD, HD))).astype(np.float32)
    freq = np.float32(10000.0) ** (-np.arange(HALF, dtype=np.float32) / np.float32(HALF))
    sel = np.zeros((FOX_HEADS, FOX_HEADS, P), np.float32)
    sel[np.arange(FOX_HEADS), np.arange(FOX_HEADS)] = 1.0
    heads = np.zeros((P, 2 * NROW - 2), np.float32)
    heads[:HD, NROW - 2] = heads[HD:, NROW - 1] = 1.0
    rows = np.kron(np.eye(NROW), np.ones((1, HD))).astype(np.float32)
    return {"k_heads": heads, "k_rows": rows, "k_ident": np.eye(P, dtype=np.float32), "k_half": half, "k_onehot": onehot,
            "k_mask": mask, "k_freq": np.broadcast_to(freq, (P, HALF)).astype(np.float32).copy(),
            "k_sel": sel}


def build(nc, I, out):
    f32, f32r, i32 = mybir.dt.float32, mybir.dt.float32r, mybir.dt.int32
    ALU, ACT = mybir.AluOpType, mybir.ActivationFunctionType
    mult, add, sub = ALU.mult, ALU.add, ALU.subtract
    ds = bass.ds

    def cols(w, c, n, k0=0, kn=KC):
        return w[k0 * P:(k0 + kn) * P, c:c + n].rearrange("(k p) n -> p k n", p=P)

    w_in, w_in2 = I["w_in"], I["w_in_2"]
    splits, directs = [], []

    def panel(name, parts):
        splits.append((name, parts))

    def chunk(name, w, c, n=P):
        panel(name, [(0, KC, n, 0, n, cols(w, c, n))])

    def ada(m, behind):
        directs.append((behind, [(0, 1, D, 0, D, cols(I["w_ada"], m // KC * D, D, m % KC, 1))]))

    for m in range(ADA_FIRST):
        ada(m, -1)
    for c in range(6):
        chunk("cq", w_in, C_CQ + c * P)
    for c in range(2):
        chunk("ckv", w_in, C_KV + c * P)
    chunk("kr", w_in, C_KR, ROPE)
    for c in range(4):
        chunk("aq", w_in, c * P)
    for c in range(4):
        chunk("ak", w_in, AW + c * P)
    for k in range(4):
        panel("av", [(0, 2, AW, 0, AW, cols(w_in, 2 * AW, AW, 2 * k, 2))])
    for k in range(6):
        panel("uq", [(0, 1, 768, 0, 768, cols(I["w_uq"], 0, 768, k, 1))])
    for k in range(2):
        panel("ukv", [(0, 1, 1024, 0, 1024, cols(I["w_ukv"], 0, 1024, k, 1))])
    for c in range(16):
        chunk("gate", w_in, C_GA + c * P)
        for m in ADA_JOB[c]:
            ada(m, len(splits) - 1 + AHEAD)
    for c in range(KC):
        panel("up", [(0, 4, P, 0, P, cols(I["w_up_a"], c * P, P, 0, 4)),
                     (512, 4, P, 0, P, cols(I["w_up_b"], c * P, P, 0, 4))])
        if c % 2:
            ada(ADA_LAST + c // 2, len(splits) - 1 + AHEAD)
    for c in range(KC):
        chunk("wo", I["w_o"], c * P)
        if c < KC // 2:
            ada(ADA_LAST + KC // 2 + c, len(splits) - 1 + AHEAD)

    def ffn_panels(f):
        splits.extend([("ffn%d" % f, None)] * (3 * FC))

    ffn_panels(0)
    for c in range(2):
        chunk("fq", w_in2, C_FQ + c * P)
    for c in range(2):
        chunk("fk", w_in2, C_FK + c * P)
    for c in range(2):
        chunk("nq", w_in2, C_NQ + c * P)
    chunk("kcvc", w_in2, C_NKV)
    panel("kskw", [(0, KC, P, 0, HD, cols(w_in2, C_NKV + 2 * HD, HD)),
                   (0, KC, P, HD, HD, cols(w_in2, C_NKV + 4 * HD, HD))])
    panel("fg", [(0, KC, 16, 0, FOX_HEADS, cols(w_in2, C_FF, FOX_HEADS)),
                 (0, KC, 16, FOX_HEADS, 12, cols(w_in2, C_NG, 12))])
    panel("vsvw", [(0, KC, P, 0, HD, cols(w_in2, C_NKV + 3 * HD, HD)),
                   (0, KC, P, HD, HD, cols(w_in2, C_NKV + 5 * HD, HD))])
    for k in range(2):
        panel("fv", [(0, 4, GROUP, 0, GROUP, cols(w_in2, C_FV, GROUP, 4 * k, 4))])
    FILL = [C_LX, C_LX + P, C_SC, C_SC + P, C_SX, C_SX + P, C_SB, C_SB + P, C_LG, C_LG + P]
    for c in FILL[:4]:
        chunk("fill", w_in2, c)
    for kv in range(2):
        for half in range(2):
            directs.append((len(splits) - 1 + AHEAD,
                            [(0, 8, P, 0, P, I["nsa_cmp_w1_2"][kv].rearrange("(k p) n -> p k n", p=P)
                              [:, 8 * half:8 * half + 8, :])]))
    for c in FILL[4:]:
        chunk("fill", w_in2, c)
    for c in range(KC):
        chunk("wout", I["w_out_2"], c * P)
    ffn_panels(1)
    panels, at = [], {}
    for n in range(-1, len(splits)):
        if n >= 0:
            at.setdefault(splits[n][0], len(panels))
            panels.append((True, splits[n][1]))
        panels += [(False, parts) for behind, parts in directs if behind == n]
    NPANEL = len(panels)
    order, count = [], [0, 0]
    for split, _ in panels:
        order.append(count[split])
        count[split] += 1

    def nth(name, k=0):
        return order[at[name]] + k

    ctx = ExitStack()
    with ctx:
        def sb(name, shape, dt=f32):
            return ctx.enter_context(nc.sbuf_tensor(name, shape, dt))

        def sem(name):
            return ctx.enter_context(nc.semaphore(name))

        raw = sb("raw", [P, RAW, PW])
        w_hi = sb("w_hi", [P, HL, PW], f32r)
        w_lo = sb("w_lo", [P, HL, PW], f32r)
        xT = sb("xT", [P, KC, SEQ])
        sq = sb("sq", [P, KC, SEQ])
        tot = sb("tot", [P, SEQ])
        totg = sb("totg", [P, SEQ])
        h_hi = sb("h_hi", [P, KC, SEQ], f32r)
        h_lo = sb("h_lo", [P, KC, SEQ], f32r)
        mix_hi = sb("mix_hi", [P, KC, SEQ], f32r)
        mix_lo = sb("mix_lo", [P, KC, SEQ], f32r)
        bias = sb("bias", [P, NB, FW])
        zb = sb("zb", [P, 2, FW])
        zc = sb("zc", [P, 2, 2, 16])
        ptb = sb("ptb", [P, 2, FW])
        qkb = sb("qkb", [MQ, 4, P])
        g_hi = sb("g_hi", [P, 2, SEQ], f32r)
        g_lo = sb("g_lo", [P, 2, SEQ], f32r)
        ident = sb("ident", [P, P])
        half1 = sb("half1", [P, P])
        ones = sb("ones", [P, SEQ])
        mask = sb("mask", [P, FW])
        va = sb("va", [P, VA_ROWS])
        vb = sb("vb", [P, VB_ROWS])
        mod = sb("mod", [P, 6, KC])
        gs = sb("gs", [P, 2, KC])
        cond = sb("cond", [P, KC])
        small = sb("small", [P, 160])
        arena = sb("arena", [P, ARENA])

        where = [0]

        def take(*shape, rows=P, start=None):
            if start is not None:
                where[0] = start
            n = int(np.prod(shape))
            v = arena[0:rows, where[0]:where[0] + n]
            where[0] += n
            assert where[0] <= ARENA, where
            names = "abcd"[:len(shape)]
            if len(shape) > 1:
                v = v.rearrange("p (%s) -> p %s" % (" ".join(names), " ".join(names)),
                                **dict(zip(names[1:], shape[1:])))
            return v

        aqT, akT = take(4, SEQ, start=0), take(4, SEQ)
        a_v = take(TT, AW)
        q_tm, k_tm = take(TT, MH, MQ), take(TT, MH, MQ)
        m_v = take(TT, MH * MV)
        kr = take(TT, 1, ROPE)
        rt = [take(TT, MH, HALF) for _ in range(4)]
        gates = take(16, SEQ)
        x_tm = take(TT, D, start=0)
        va_rows = take(P, rows=VA_ROWS)
        vb_rows = take(P, rows=VB_ROWS)
        onehot = take(2, FW, rows=BUCKETS + 1)
        relc = take(NB, rows=BUCKETS + 1)
        ang, turns, arg = (take(TT, HALF) for _ in range(3))
        acc01 = take(2, D)
        frow = [take(FW, rows=n, start=ARENA - x * FW) for n, x in ((A_HEADS, 2), (NSA_HEADS, 1))]
        sg, hf = take(2, SEQ, start=0), take(2, SEQ)
        sqg = take(KC, SEQ)
        where[0] -= KC * SEQ
        fqT, fkT = take(2, SEQ), take(2, SEQ)
        f_v = take(TT, GROUP)
        nqT = take(2, SEQ)
        kcvc, kcvc_x, kskw, kskw_x = (take(SEQ) for _ in range(4))
        n_v = take(TT, 2, HD)
        fg = take(TT, 16)
        gate2 = take(TT, 12)
        gb_row = take(12)
        xb = take(2, 16, NCMP)
        crow = take(FOX_HEADS, SEQ)
        dec = take(FOX_HEADS, FW)
        cf = take(3, SEQ, rows=FOX_HEADS)
        selb = take(FOX_HEADS, P, rows=FOX_HEADS)
        fbias = take(1, rows=FOX_HEADS)
        hid = take(2, 16)
        kcT = take(16)
        kcq = take(16)
        v_c = take(HD, rows=16)
        w2k = take(2, HD)
        w2v = take(HD)
        lx = take(2, SEQ + 3)
        lg, s_b, s_c = take(2, SEQ), take(2, SEQ), take(2, SEQ)
        sx = take(2, SEQ + 2)
        lw = take(2, 2, P)
        heads = take(2 * NROW - 2)
        rinv = take(SEQ, rows=NROW)
        free = bias[:, 0:A_HEADS, :].rearrange("p a b -> p (a b)")
        yT = free[:, 0:KC * SEQ].rearrange("p (a b) -> p a b", b=SEQ)
        xc = free[:, 8 * SEQ:10 * SEQ].rearrange("p (a b) -> p a b", b=SEQ)
        ra = free[:, 10 * SEQ:12 * SEQ].rearrange("p (a b) -> p a b", b=SEQ)
        ia = crow[:, 0:2, :]
        rows14 = free[0:NROW, 4 * SEQ:4 * SEQ + NROW * HD]

        def col(c, n=1, rows=P):
            return small[0:rows, c:c + n]
        eps_c, hpi_c = col(0), col(1)
        pos_f = col(4, 2)
        invq, invkv = col(6, 2), col(8, 2)
        nm, den, rec = small[:, 12:16], small[:, 16:20], small[:, 20:24]
        mx = small[:, 24:28]
        ccol = small[:, 28:36]
        rms, inv = small[:, 64:66], small[:, 66:68]
        rms2, inv2, ms2 = small[:, 68:70], small[:, 70:72], small[:, 72:74]
        warm, yrms = col(74), small[:, 84:92]
        gg = small[:, 76:84]
        spt = [small[:, 40 + 2 * i:42 + 2 * i] for i in range(8)]
        pos_i = sb("pos_i", [P, 2], i32)
        freq = sb("freq", [P, HALF])
        cosT, sinT = sb("cosT", [P, TT, HALF]), sb("sinT", [P, TT, HALF])

        ps = [ctx.enter_context(nc.psum_tensor(f"ps{i}", [P, 512], f32)) for i in range(8)]
        LIN = [ps[4], ps[5]]
        MOD = ps[6][:, 0:48]
        YSUM = ps[6][:, 128:136]
        NSUM, NSUM2 = ps[7][:, 0:2], ps[7][:, 2:4]
        NRM, NRM2 = ps[7][:, SEQ:512], ps[7][:, 0:SEQ]
        frow_dram = nc.dram_tensor("head_rows", [P, NB * FW], f32, kind="Internal").ap()

        raw_in = [sem(f"raw_in{i}") for i in range(RAW)]
        hi_done, lo_done, panel_used = sem("hi_done"), sem("lo_done"), sem("panel_used")
        ada_used, cmp_used = sem("ada_used"), sem("cmp_used")
        S = {}

        def s(name):
            if name not in S:
                S[name] = sem(name)
            return S[name]

        class Line:

            def __init__(self, eng, name):
                self.eng, self.own, self.n = eng, s(name), {}
                self.last = None

            def __call__(self, ins, name=None):
                sm = self.own if name is None else s(name)
                ins.then_inc(sm, 1)
                self.n[name] = self.n.get(name, 0) + 1
                self.last = (sm, self.n[name])

            def settle(self):
                self.eng.wait_ge(*self.last)

            def skip(self, name, k):
                self.n[name] = self.n.get(name, 0) + k

        loads = {
            "in_x": [(x_tm, I["x"].rearrange("(t p) d -> p t d", p=P))],
            "in_va": [(va_rows[0:48, :], I["b_ada"].rearrange("(r p) -> r p", p=P)),
                      (va_rows[48:56, :], I["g_mix"].rearrange("(r p) -> r p", p=P)),
                      (va_rows[56:64, :], I["c"].rearrange("(r p) -> r p", p=P))],
            "in_id": [(ident[:, :], I["k_ident"])],
            "in_rel": [(onehot, I["k_onehot"]),
                       (relc[0:BUCKETS, 0:A_HEADS], I["rel_bias"].rearrange("h b -> b h")),
                       (relc[0:BUCKETS, A_HEADS:NB], I["rel_bias_2"])],
            "in_pos": [(pos_i[:, :], I["positions"].rearrange("(t p) -> p t", p=P)),
                       (freq[:, :], I["k_freq"])],
            "in_mask": [(mask[:, :], I["k_mask"]), (half1[:, :], I["k_half"])],
        }

        def vrow(name, rows=None):
            r = VB[name]
            src = I[name]
            return (vb_rows[r:r + src.shape[0] // P, :], src.rearrange("(r p) -> r p", p=P))
        loads["in_vb"] = [vrow(n) for n in ("g_ffn", "g_final", "norm_mix_2", "norm_ffn_2", "out_norm_2",
                                            "g_q_lora", "g_kv_lora", "lru_conv_b_2", "lru_b_gates_2",
                                            "lru_lambda_2", "lru_conv_w_2", "sc_conv_w_2")]
        fqk, nqk = I["fox_qk_norm_2"], I["nsa_qk_norm_2"]
        for n, (a, b) in {"fox_q": (fqk[0:1], fqk[0:1]), "fox_k": (fqk[1:2], fqk[1:2]),
                          "nsa_q": (nqk[0:1], nqk[0:1]), "nsa_kskw": (nqk[2:3], nqk[3:4]),
                          "nsa_kc": (nqk[1:2], nqk[1:2])}.items():
            for x, y in enumerate((a, b)):
                loads["in_vb"].append((vb_rows[VB[n]:VB[n] + 1, x * HD:(x + 1) * HD], y))
        loads["in_vb"].append((vb_rows[VB["pos"]:VB["pos"] + 32, :],
                               I["nsa_cmp_pos_2"].rearrange("(r p) -> r p", p=P)))
        loads2 = {
            "in_heads": [(heads, I["k_heads"]), (rows14, I["k_rows"])],
            "in_b2": [(selb, I["k_sel"]), (fbias, I["fox_f_bias_2"]),
                      (gb_row, I["nsa_gate_bias_2"].partition_broadcast(P)),
                      (w2k[:, 0, :], I["nsa_cmp_w2_2"][0]), (w2k[:, 1, :], I["nsa_cmp_w2_2"][0]),
                      (w2v, I["nsa_cmp_w2_2"][1])],
            "in_lw": [(lw[64 * (h % 2):64 * (h % 2) + 64, g, h // 2, 64 * (h % 2):64 * (h % 2) + 64],
                       I["lru_w_gates_2"][g, h]) for g in range(2) for h in range(4)],
        }

        def arrived(eng, name):
            eng.wait_ge(s(name), 16 * len((loads | loads2)[name]))

        JOBS = [("A", h) for h in range(A_HEADS)] + [("M", h) for h in range(MH)]
        JOBS2 = [("F", h) for h in range(FOX_HEADS)]
        for h in range(NSA_HEADS):
            JOBS2 += [("S", h), ("W", h), ("C", h)]
        N1, N2 = len(JOBS), len(JOBS2)
        ADA_SUM = {next(c for c in range(N1) if KC * (g + 1) - 1 in ADA_JOB[c]) + 1: g for g in (2, 3, 4)}
        ALL = JOBS + JOBS2
        OUT = []
        for k, h in ALL:
            OUT.append((OUT[-1] + (k not in "WC")) if OUT else 0)
        closes = [g + 1 == len(ALL) or OUT[g + 1] != OUT[g] for g in range(len(ALL))]
        outputs, freed = [], []
        lin_freed = [0, 0]

        def output(name, k=0, free=None):
            b = len(outputs) % 2
            if free is None:
                lin_freed[b] += 1
                free = ("lin_free%d" % b, lin_freed[b])
            outputs.append(nth(name, k))
            freed.append(free)
            return len(outputs) - 1

        L = {}
        for name, n in (("cq", 6), ("ckv", 2), ("kr", 1), ("aq", 4), ("ak", 4)):
            L[name] = [output(name, c) for c in range(n)]
        L["av"] = [output("av", 3) for _ in range(TT)]
        L["gate"] = [output("gate", c) for c in range(16)]
        L["up"] = [output("up", c) for c in range(KC)]
        L["wo"] = [output("wo", c, ("x_ready", c + 1)) for c in range(KC)]
        L["ffn0"] = [output("ffn0", 0 if j == 0 else 3 * j - 1, ("hf_done", j + 1)) for j in range(FC)]
        for name, n in (("fq", 2), ("fk", 2), ("nq", 2), ("kcvc", 1), ("kskw", 1), ("fg", 1), ("vsvw", 1)):
            L[name] = [output(name, c) for c in range(n)]
        L["fv"] = [output("fv", 1) for _ in range(TT)]
        L["fill"] = [output("fill", c) for c in range(len(FILL))]
        L["wout"] = [output("wout", c, ("x_ready", 24 + c + 1)) for c in range(KC)]
        L["ffn1"] = [output("ffn1", 0 if j == 0 else 3 * j - 1, ("hf_done", FC + j + 1)) for j in range(FC)]

        def lin(l, n=SEQ, a=0):
            return LIN[l % 2][:, a:a + n]

        def bank_of(f, j):
            return LIN[(L["ffn%d" % f][0] + j) % 2]

        def await_out(eng, l):
            eng.wait_ge(panel_used, outputs[l] + 1)

        def free_name(l):
            return "lin_free%d" % (l % 2)

        def vcol(name, c=0, n=1):
            return vb[:, VB[name] + c:VB[name] + c + n]

        QK2 = [("fq", 0, fqT[:, 0, :], "fox_q"), ("fq", 1, fqT[:, 1, :], "fox_q"),
               ("fk", 0, fkT[:, 0, :], "fox_k"), ("fk", 1, fkT[:, 1, :], "fox_k"),
               ("nq", 0, nqT[:, 0, :], "nsa_q"), ("nq", 1, nqT[:, 1, :], "nsa_q"),
               ("kskw", 0, kskw, "nsa_kskw")]
        FILL_TO = [lx[:, 0, 3:], lx[:, 1, 3:], s_c[:, 0, :], s_c[:, 1, :], sx[:, 0, 2:], sx[:, 1, 2:],
                   s_b[:, 0, :], s_b[:, 1, :], lg[:, 0, :], lg[:, 1, :]]
        Y_ORDER = (2, 3, 4, 5, 6, 7, 0, 1)
        EARLY = 4

        def o_region(o):
            r = HD * (o % 2)
            return ps[7][r:r + HD, SEQ * ((o // 2) % 2):SEQ * ((o // 2) % 2) + SEQ]

        def o_rows(buf, o):
            r = HD * (o % 2)
            return buf[r:r + HD, o // 2, :]

        def ada_acc(g):
            if g < 2:
                return acc01[:, g, :]
            return {2: sq[:, 0:4, :], 3: sq[:, 4:8, :], 4: sq[:, 0:4, :], 5: aqT}[g].rearrange("p a b -> p (a b)")

        def z_parts(g):
            if ALL[g][0] == "C":
                return [zc[:, g % 2, 0, 0:NCMP0], zc[:, g % 2, 1, 0:NCMP]]
            return [zb[:, g % 2, 0:P], zb[:, g % 2, P:FW]]

        def pair(buf, g):
            return buf[:, 2 * (g % 2):2 * (g % 2) + 2]

        def hi_lo(m, a, n):
            return w_hi[:, m % HL, a:a + n], w_lo[:, m % HL, a:a + n]

        def f_pos(what, j):
            if what == "d":
                return 3 * j + 4 if j < FC - 1 else 3 * FC - 1
            return (0 if j == 0 else 3 * j - 1) + (what == "u")

        def f_src(f, what, j):
            w = ("w_gate", "w_up", "w_down") if f == 0 else ("w_gate_up_2", "w_gate_up_2", "w_down_2")
            if what == "d":
                return 1, D, I[w[2]][ds(j * P, P), :].rearrange("(k p) n -> p k n", p=P)
            base = D_FF if (f == 1 and what == "u") else 0
            src = I[w["gu".index(what)]][:, ds(j * P + base, P)]
            return KC, P, src.rearrange("(k p) n -> p k n", p=P)

        raw_count, raised = [], [0] * RAW
        for n, (_, parts) in enumerate(panels):
            raised[n % RAW] += 16 * (len(parts) if parts else 1)
            raw_count.append(raised[n % RAW])
        index_of = [n for n in range(NPANEL) if panels[n][0]]
        direct_of = [n for n in range(NPANEL) if not panels[n][0]]
        widths = [max(a + kn * c for a, kn, c, _, _, _ in panels[n][1]) if panels[n][1] else PW
                  for n in index_of]
        NS = len(index_of)
        ITER = (FC - 4) // 2
        assert RAW == 6 and HL == 6

        ctx.enter_context(nc.allow_non_contiguous_dma(reason="a few small vectors laid out by partition"))
        block = ctx.enter_context(nc.Block())

        @block.sync
        def _(sp):
            def load(n, parts, i=0):
                if n >= RAW:
                    o = n - RAW
                    if panels[o][0]:
                        sp.wait_ge(lo_done, order[o] + 1 + i * 6)
                    else:
                        sp.wait_ge(*((ada_used, order[o] + 1) if order[o] < ADA else (cmp_used, order[o] + 1 - ADA)))
                for a, kn, c, off, w, src in parts:
                    dst = raw[:, n % RAW, a:a + kn * c].rearrange("p (k n) -> p k n", n=c)[:, :, off:off + w]
                    sp.dma_start(dst, src).then_inc(raw_in[n % RAW], 16)

            def ffn(f):
                n0 = at["ffn%d" % f]

                def one(n, what, j, i=0):
                    kn, c, src = f_src(f, what, j)
                    load(n, [(0, kn, c, 0, c, src)], i)
                one(n0, "g", 0)
                one(n0 + 1, "u", 0)
                for j in (1, 2):
                    one(n0 + f_pos("g", j), "g", j)
                    one(n0 + f_pos("u", j), "u", j)
                    one(n0 + f_pos("d", j - 1), "d", j - 1)
                with sp.Fori(0, ITER) as i:
                    for j in (3, 4):
                        one(n0 + f_pos("g", j), "g", i * 2 + j, i)
                        one(n0 + f_pos("u", j), "u", i * 2 + j, i)
                        one(n0 + f_pos("d", j - 1), "d", i * 2 + (j - 1), i)
                e = n0 + 3 * FC - 4
                one(e, "g", FC - 1)
                one(e + 1, "u", FC - 1)
                one(e + 2, "d", FC - 2)
                one(e + 3, "d", FC - 1)

            n = 0
            while n < NPANEL:
                if panels[n][1] is None:
                    ffn(int(n != at["ffn0"]))
                    n += 3 * FC
                else:
                    load(n, panels[n][1])
                    n += 1
            for t in range(TT):
                sp.wait_ge(s("y_copied"), 2 * (t + 1))
                sp.dma_start(out[t * P:(t + 1) * P, :], arena[:, t * D:(t + 1) * D]).then_inc(s("out_done"), 16)
            sp.wait_ge(s("out_done"), 16 * TT)

        class Splitter:

            def __init__(self, part):
                self.part, self.next = part, 0

            def ahead(self, m):
                while self.next < min(m + 1 + AHEAD, NS):
                    self.part(self.next, 0)
                    self.next += 1

        @block.scalar
        def _(act):
            A = nc.scalar.activation
            line = Line(act, "act_step")

            def split_hi(m, i):
                n = index_of[m]
                act.wait_ge(raw_in[n % RAW], raw_count[n] + i * 16)
                if m >= HL:
                    act.wait_ge(panel_used, m - HL + 1 + i * 6)
                w = widths[m]
                A(w_hi[:, m % HL, 0:w], raw[:, n % RAW, 0:w], ACT.Copy).then_inc(hi_done, 1)
            split = Splitter(split_hi)

            for name in ("in_id", "in_va", "in_x"):
                for dst, src in loads[name]:
                    act.dma_start(dst, src).then_inc(s(name), 16)
            act.wait_ge(s("va_t"), 1)
            line(A(va[:, :], ps[5][:, 0:VA_ROWS], ACT.Copy), "va_ready")
            line.settle()
            line(A(cond[:, :], va[:, 56:64], ACT.Silu), "cond_ready")
            for b in range(4):
                act.wait_ge(s("x_t"), b + 1)
                line(A(xT[:, 2 * b:2 * b + 2, :].rearrange("p a b -> p (a b)"), ps[b][:, :], ACT.Copy), "x_copied")
            line.settle()

            def square(c, base=None):
                if base is not None:
                    act.wait_ge(s("x_ready"), base + c + 1)
                line(A(sq[:, c, :], xT[:, c, :], ACT.Square), "sq_ready")

            def root(k):
                act.wait_ge(s("ss_done"), k + 1)
                line(A(rms, NSUM, ACT.Sqrt, scale=1.0 / D, bias=eps_c), "rms_ready")

            def prepare_root():
                line(A(warm, eps_c, ACT.Sqrt))

            def highs(k, shift=None):
                for c in range(KC):
                    act.wait_ge(s("h_ready"), 8 * k + c + 1)
                    if shift is None:
                        line(A(h_hi[:, c, :], sq[:, c, :], ACT.Copy), "h_hi")
                    else:
                        line(A(h_hi[:, c, :], sq[:, c, :], ACT.Identity, bias=mod[:, shift, c:c + 1]), "h_hi")

            for c in range(KC):
                square(c)
            act.wait_ge(s("const_ready"), 1)
            root(0)
            for n in range(2):
                act.wait_ge(s("frow_mm"), n + 1)
                line(A(frow[n], ps[n][0:frow[n].shape[0], 0:FW], ACT.Copy), "frow_copied")
            act.wait_ge(s("arg_ready"), 1)
            line(A(sinT[:, :, :], ang, ACT.Sin))
            line(A(cosT[:, :, :], arg, ACT.Sin, scale=-1.0, bias=hpi_c), "trig_ready")
            act.wait_ge(s("vb_t"), 1)
            line(A(vb[:, :], ps[2][:, 0:VB_ROWS], ACT.Copy), "vb_ready")
            split.ahead(-1)
            highs(0, shift=0)

            act.wait_ge(s("h_lo"), 8)
            for c in range(8):
                l = (L["cq"] + L["ckv"])[c]
                split.ahead(outputs[l])
                await_out(act, l)
                line(A(sq[:, c, :], lin(l), ACT.Square), "lat_sq")
                line(A(mix_hi[:, c, :], lin(l), ACT.Copy, scale=vcol("g_q_lora", c)), "lat_hi")
                if c == 1:
                    act.wait_ge(s("frow_copied"), 2)
                    rows = frow_dram.rearrange("p (h i) -> h p i", i=FW)
                    for v, (h0, h1) in zip(frow, ((0, A_HEADS), (A_HEADS, NB))):
                        act.dma_start(rows[h0:h1], v.unsqueeze(1).to_broadcast([h1 - h0, P, FW])).then_inc(s("frow_out"), 16)
            l = L["kr"][0]
            split.ahead(outputs[l])
            await_out(act, l)
            line(A(kr.rearrange("p t a r -> p (t a r)"), lin(l, TT * ROPE), ACT.Copy), free_name(l))
            for c, l in enumerate(L["aq"] + L["ak"]):
                split.ahead(outputs[l])
                await_out(act, l)
                line(A((aqT if c < 4 else akT)[:, c % 4, :], lin(l), ACT.Copy), free_name(l))
                if c == 2:
                    act.wait_ge(s("frow_out"), 32)
                    for a, n, off in ((P, SEQ, P - 1), (0, P, SEQ - 1)):
                        act.dma_start(bias[:, :, a:a + n],
                                      bass.AP(frow_dram.tensor, off, [[NB * FW - 1, P], [FW, NB], [1, n]]))\
                            .then_inc(s("bias_in"), 16)
            split.ahead(nth("av", 3))
            for t, l in enumerate(L["av"]):
                await_out(act, l)
                line(A(a_v[:, t, :], lin(l, 512), ACT.Copy), free_name(l))
            act.wait_ge(s("lat_ss"), 1)
            for q, n in enumerate((Q_LORA, KV_LORA)):
                line(A(small[:, 56 + 2 * q:58 + 2 * q], ps[7][:, 2 * q:2 * q + 2], ACT.Sqrt, scale=1.0 / n,
                       bias=eps_c), "lat_rms")
            split.ahead(nth("uq", 5))
            act.wait_ge(s("lat_inv"), 1)
            act.wait_ge(panel_used, nth("uq", 5) + 1)
            for b in range(4):
                t, q = b // 2, b % 2
                line(A(q_tm[:, t, 4 * q:4 * q + 4, :].rearrange("p a b -> p (a b)"), ps[b][:, 0:384], ACT.Copy,
                       scale=invq[:, t:t + 1]), "q_copied")
            split.ahead(nth("ukv", 1))
            act.wait_ge(panel_used, nth("ukv", 1) + 1)
            for b in range(4):
                t, q = b // 2, b % 2
                v = ps[b][:, :].rearrange("p (h c) -> p h c", c=NOPE + MV)
                line(A(m_v[:, t, 256 * q:256 * q + 256].rearrange("p (h c) -> p h c", c=MV), v[:, :, NOPE:], ACT.Copy,
                       scale=invkv[:, t:t + 1]), "v_copied")

            def exps(g):
                act.wait_ge(s("z_ready"), g + 1)
                for t, z in enumerate(z_parts(g)):
                    line(A(z, z, ACT.Exp, bias=pair(nm, g)[:, t:t + 1], accum_out=pair(den, g)[:, t:t + 1]), "e_ready")

            def pt_copy(g):
                act.wait_ge(s("pt_done"), g + 1)
                if g >= 2:
                    act.wait_ge(s("pv_done"), g - 1)
                if ALL[g][0] == "C":
                    line(A(ptb[0:NCMP, g % 2, 0:SEQ], ps[2][0:NCMP, 0:SEQ], ACT.Copy), "pt_copied")
                else:
                    line(A(ptb[:, g % 2, :], ps[2][:, 0:FW], ACT.Copy), "pt_copied")

            def o_copy(g):
                if closes[g]:
                    act.wait_ge(s("pv_done"), g + 1)
                    o = OUT[g]
                    if g < N1:
                        line(A(o_rows(mix_hi, o), o_region(o), ACT.Copy), "o_hi")
                    else:
                        line(A(o_rows(yT, 8 + o - 16), o_region(o), ACT.Copy), "o_hi")

            def qk_copy(h):
                act.wait_ge(s("qkt_done"), h + 1)
                if h >= 1:
                    act.wait_ge(s("s_done"), A_HEADS + h)
                line(A(qkb[:, :, :].rearrange("p a b -> p (a b)"), ps[3][0:MQ, :], ACT.Copy), "qk_copied")

            act.wait_ge(s("lam_abs"), 1)
            line(A(spt[0], spt[5], ACT.Exp, scale=-1.0), "lam_exp")
            for g in range(N1 + 2):
                if g < N1:
                    split.ahead(nth("gate", g))
                    exps(g)
                if A_HEADS <= g + 2 < N1:
                    qk_copy(g + 2 - A_HEADS)
                if g < N1:
                    l = L["gate"][g]
                    await_out(act, l)
                    line(A(gates[:, g, :], lin(l), ACT.Copy), free_name(l))
                if 1 <= g <= N1:
                    pt_copy(g - 1)
                if g >= 2:
                    o_copy(g - 2)
            split.ahead(nth("up", 0))
            for c in range(KC):
                for k in (c, 8 + c):
                    line(A(gates[:, k, :], gates[:, k, :], ACT.Sigmoid), "sig_done")
            for c in range(KC + 1):
                split.ahead(nth("up", c) if c < KC else nth("wo", 0))
                if c >= 1:
                    act.wait_ge(s("merged"), c)
                    line(A(h_hi[:, c - 1, :], sq[:, c - 1, :], ACT.Copy), "m_hi")
            prepare_root()
            for c in range(KC):
                split.ahead(nth("wo", c))
                act.wait_ge(s("m_lo"), 8)
                square(c, 0)
            root(1)
            highs(1, shift=3)

            def ffn(f):
                m0 = nth("ffn%d" % f)
                assert split.next == m0 + AHEAD, (split.next, m0)

                def hidden(j, i, more):
                    J = FC * f + j
                    for m in more[:1]:
                        split_hi(m, i)
                    act.wait_ge(panel_used, m0 + f_pos("u", j) + 1 + i * 6)
                    line(A(sg[:, j % 2, :], bank_of(f, j)[:, 0:SEQ], ACT.Silu), "silu_done")
                    for m in more[1:2]:
                        split_hi(m, i)
                    act.wait_ge(s("hf_done"), J + 1 + i * 2)
                    if j >= 2:
                        act.wait_ge(panel_used, m0 + f_pos("d", j - 2) + 1 + i * 6)
                    line(A(g_hi[:, j % 2, :], hf[:, j % 2, :], ACT.Copy), "g_hi")
                    for m in more[2:]:
                        split_hi(m, i)
                e = split.next
                hidden(0, 0, [e, e + 1])
                for j in (1, 2):
                    hidden(j, 0, [e + 3 * j - 1 + k for k in range(3)])
                with act.Fori(0, ITER) as i:
                    for j in (3, 4):
                        hidden(j, i, [e + 3 * j - 1 + k for k in range(3)])
                line.skip("silu_done", 2 * (ITER - 1))
                line.skip("g_hi", 2 * (ITER - 1))
                split.next = e + 3 * FC - 4
                more = [m for m in range(split.next, split.next + 3) if m < NS]
                hidden(FC - 1, 0, more)
                split.next += len(more)
            ffn(0)
            prepare_root()
            for c in range(KC):
                square(c, 8)
                line(A(sqg[:, c, :], xT[:, c, :], ACT.Square, scale=vcol("g_final", c)), "sqg_ready")
            root(2)
            act.wait_ge(s("ms2_ready"), 1)
            line(A(rms2, ms2, ACT.Sqrt, scale=1.0 / D, bias=eps_c), "rms2_ready")
            highs(2)

            act.wait_ge(s("h_lo"), 24)
            for q, (name, c, dst, _) in enumerate(QK2[:6]):
                l = L[name][c]
                split.ahead(outputs[l])
                await_out(act, l)
                line(A(sq[:, q, :], lin(l), ACT.Square), "qk_sq")
                line(A(dst, lin(l), ACT.Copy), free_name(l))
            l = L["kcvc"][0]
            split.ahead(outputs[l])
            await_out(act, l)
            line(A(kcvc, lin(l), ACT.Copy), free_name(l))
            l = L["kskw"][0]
            split.ahead(outputs[l])
            await_out(act, l)
            line(A(sq[:, 6, :], lin(l), ACT.Square), "qk_sq")
            line(A(kskw, lin(l), ACT.Copy), free_name(l))
            l = L["fg"][0]
            split.ahead(outputs[l])
            await_out(act, l)
            line(A(fg.rearrange("p t a -> p (t a)"), lin(l, TT * 16), ACT.Copy), free_name(l))
            l = L["vsvw"][0]
            split.ahead(outputs[l])
            await_out(act, l)
            line(A(n_v.rearrange("p t a b -> p (t a b)"), lin(l, TT * P), ACT.Copy), free_name(l))
            split.ahead(nth("fv", 1))
            for t, l in enumerate(L["fv"]):
                await_out(act, l)
                line(A(f_v[:, t, :], lin(l, GROUP), ACT.Copy), free_name(l))
            act.wait_ge(s("qk_ss"), 1)
            line(A(rinv, ps[0][0:NROW, 0:SEQ], ACT.Sqrt, scale=1.0 / HD, bias=eps_c[0:NROW]), "qk_rms")
            for q in range(EARLY):
                l = L["fill"][q]
                split.ahead(outputs[l])
                await_out(act, l)
                line(A(FILL_TO[q], lin(l), ACT.Copy), free_name(l))
            act.wait_ge(s("f_abs"), 1)
            line(A(cf[:, 1, :], cf[:, 1, :], ACT.Exp, scale=-1.0))
            line.settle()
            line(A(cf[:, 1, :], cf[:, 1, :], ACT.Ln, bias=ones[0:FOX_HEADS, 0:1]), "f_log")
            act.wait_ge(cmp_used, 4)
            line(A(hid[:, :, 0:NCMP], ps[7][:, 0:32].rearrange("p (a b) -> p a b", b=16)[:, :, 0:NCMP],
                   ACT.Gelu_apprx_tanh), "hid_ready")
            act.wait_ge(s("kc_mm"), 1)
            line(A(kcT[:, 0:NCMP], ps[7][:, 32:32 + NCMP], ACT.Copy))
            line(A(kcq[:, 0:NCMP], ps[7][:, 32:32 + NCMP], ACT.Square), "kc_sq")
            act.wait_ge(s("vc_mm"), 1)
            line(A(v_c[0:NCMP, :], ps[6][0:NCMP, 64:64 + HD], ACT.Copy), "vc_ready")
            act.wait_ge(s("kc_ss"), 1)
            line(A(kcq[:, 0:NCMP], ps[7][:, 48:48 + NCMP], ACT.Sqrt, scale=1.0 / HD, bias=eps_c), "kc_rms")

            act.wait_ge(s("gate_sum"), 1)
            line(A(gate2, gate2, ACT.Sigmoid), "gate2_ready")
            for q in range(4):
                act.wait_ge(s("lru_mm"), 2 * (q // 2) + 2)
                line(A((ra, ia)[q // 2][:, q % 2, :], ps[q // 2][:, SEQ * (q % 2):SEQ * (q % 2) + SEQ], ACT.Sigmoid,
                       bias=vcol("lru_b_gates_2", q)), "lru_sig")
            line.settle()
            act.wait_ge(s("lru_c"), 1)
            for c in range(2):
                line(A(yT[:, c, :], ra[:, c, :], ACT.Tanh, scale=spt[7][:, c:c + 1]), "lru_tanh")
            for c in range(2):
                line(A(ra[:, c, :], ra[:, c, :], ACT.Exp, scale=spt[6][:, c:c + 1]), "lru_a")

            for g in range(N1, N1 + N2 + 2):
                q = EARLY + g - N1
                if g < N1 + N2:
                    if q < len(FILL):
                        split.ahead(nth("fill", q))
                    exps(g)
                    if q < len(FILL):
                        l = L["fill"][q]
                        await_out(act, l)
                        line(A(FILL_TO[q], lin(l), ACT.Copy), free_name(l))
                if N1 < g <= N1 + N2:
                    pt_copy(g - 1)
                if g == N1 + N2:
                    line(A(lg, lg, ACT.Gelu_apprx_tanh), "lg_ready")
                    act.wait_ge(s("lru_w"), 1)
                    line(A(yT[:, 0:2, :], yT[:, 0:2, :], ACT.Sqrt), "lru_sqrt")
                if g >= N1 + 2:
                    o_copy(g - 2)
            for n, c in enumerate(Y_ORDER):
                if n == 0:
                    act.wait_ge(s("yb_ready"), 1)
                if n == 2:
                    act.wait_ge(s("o_hi"), 24)
                if n == 6:
                    act.wait_ge(s("ya_ready"), 1)
                line(A(sq[:, c, :], yT[:, c, :], ACT.Square), "y_sq")
            act.wait_ge(s("y_ss"), 4)
            line(A(yrms, YSUM, ACT.Sqrt, scale=1.0 / GROUP, bias=eps_c), "y_rms")
            for n, c in enumerate(Y_ORDER):
                act.wait_ge(s("y_ready"), n + 1)
                line(A(mix_hi[:, c, :], yT[:, c, :], ACT.Copy), "y_hi")
            for c in range(KC):
                split.ahead(nth("wout", c))
                if c == 0:
                    act.wait_ge(s("y_lo"), 8)
                square(c, 24)
            root(3)
            highs(3)
            ffn(1)
            for b in range(4):
                act.wait_ge(s("y_t"), b + 1)
                line(A(arena[:, b * 512:(b + 1) * 512], ps[b][:, :], ACT.Copy), "y_copied")

        @block.vector
        def _(dve):
            V = nc.vector
            line = Line(dve, "dve_step")
            stt = V.scalar_tensor_tensor

            def split_lo(m, i):
                n, w = index_of[m], widths[m]
                dve.wait_ge(hi_done, m + 1 + i * 6)
                V.tensor_tensor(w_lo[:, m % HL, 0:w], raw[:, n % RAW, 0:w], w_hi[:, m % HL, 0:w].bitcast(f32),
                                sub).then_inc(lo_done, 1)
            split = Splitter(split_lo)

            line(V.memset(ones[:, :], 1.0))
            line(V.memset(eps_c, EPS))
            line(V.memset(hpi_c, math.pi / 2))
            line(V.memset(relc[BUCKETS:BUCKETS + 1], 1.0))
            line(V.memset(zc[:, :, :, :], 0.0), "const_ready")
            arrived(dve, "in_pos")
            line(V.tensor_copy(pos_f, pos_i[:, :]))
            line.settle()
            for t in range(TT):
                line(V.tensor_scalar(ang[:, t, :], freq[:, :], pos_f[:, t:t + 1], None, mult))
            line.settle()
            line(V.tensor_scalar(turns, ang, 1.0 / (2 * math.pi), MAGIC, mult, add))
            line.settle()
            line(V.tensor_scalar(turns, turns, MAGIC, None, sub))
            for c in (C1, C2, C3):
                line.settle()
                line(stt(out=ang, in0=turns, scalar=-c, in1=ang, op0=mult, op1=add))
            line.settle()
            line(V.tensor_scalar(ang, ang, 3.1415925, -3.1415925, ALU.min, ALU.max))
            line.settle()
            line(stt(out=arg, in0=ang, scalar=-1.0, in1=ang, op0=mult, op1=ALU.max), "arg_ready")

            def inverse(k):
                dve.wait_ge(s("rms_ready"), k + 1)
                line(V.reciprocal(inv, rms), "inv_col")

            def total(c, k):
                if c >= 1:
                    dve.wait_ge(s("sq_ready"), 8 * k + c + 1)
                    line.settle()
                    line(V.tensor_tensor(tot[:, :], sq[:, 0, :] if c == 1 else tot[:, :], sq[:, c, :], add),
                         "tot_ready" if c == KC - 1 else None)

            def modulate(g, n=1):
                dve.wait_ge(s("mod_sum"), g + n)
                line(V.tensor_tensor(mod[:, g:g + n, :].rearrange("p a b -> p (a b)"), MOD[:, 8 * g:8 * (g + n)],
                                     va[:, 8 * g:8 * (g + n)], add))
                line.settle()

            def ada(m):
                n, g, k = direct_of[m], m // KC, m % KC
                acc, w = ada_acc(g), raw[:, direct_of[m] % RAW, :]
                dve.wait_ge(raw_in[n % RAW], raw_count[n])
                if k == 0:
                    ins = V.tensor_scalar(acc, w, cond[:, k:k + 1], None, mult)
                else:
                    dve.wait_ge(ada_used, m)
                    ins = stt(out=acc, in0=w, scalar=cond[:, k:k + 1], in1=acc, op0=mult, op1=add)
                ins.then_inc(ada_used, 1)

            dve.wait_ge(s("cond_ready"), 1)
            for m in range(2 * KC):
                ada(m)
                if m < KC:
                    total(m, 0)
                if m == KC:
                    inverse(0)
            split.ahead(-AHEAD)
            modulate(0, 2)
            line(stt(out=gs[:, 0, :], in0=mod[:, 1, :], scalar=1.0, in1=va[:, 48:56], op0=add, op1=mult))

            def normed(k, gain, shift=None):
                def low(c):
                    dve.wait_ge(s("h_hi"), 8 * k + c + 1)
                    hi = h_hi[:, c, :].bitcast(f32)
                    if shift is None:
                        line(V.tensor_tensor(h_lo[:, c, :], sq[:, c, :], hi, sub), "h_lo")
                    else:
                        line(stt(out=h_lo[:, c, :], in0=sq[:, c, :], scalar=mod[:, shift, c:c + 1], in1=hi,
                                 op0=add, op1=sub), "h_lo")
                dve.wait_ge(s("inv_ready"), k + 1)
                for c in range(KC):
                    line(stt(out=sq[:, c, :], in0=xT[:, c, :], scalar=gain[:, c:c + 1], in1=NRM, op0=mult,
                             op1=mult), "h_ready")
                    if c >= 2:
                        low(c - 2)
                low(KC - 2)
                low(KC - 1)
            dve.wait_ge(s("x_copied"), 4)
            line.settle()
            normed(0, gs[:, 0, :], 0)
            split.ahead(-1)

            dve.wait_ge(s("vb_ready"), 1)
            line(V.tensor_tensor(gg, vcol("g_final", 0, 8), vcol("norm_mix_2", 0, 8), mult))
            lam = vcol("lru_lambda_2", 0, 2)
            line(stt(out=spt[5], in0=lam, scalar=-1.0, in1=lam, op0=mult, op1=ALU.max), "lam_abs")
            for c, l in enumerate(L["cq"] + L["ckv"]):
                split.ahead(outputs[l])
                dve.wait_ge(s("lat_hi"), c + 1)
                line(stt(out=mix_lo[:, c, :], in0=lin(l), scalar=vcol("g_q_lora", c), in1=mix_hi[:, c, :].bitcast(f32),
                         op0=mult, op1=sub), free_name(l))
            split.ahead(nth("av", 3))
            dve.wait_ge(s("lat_rms"), 2)
            line(V.reciprocal(small[:, 6:10], small[:, 56:60]), "lat_inv")
            split.ahead(nth("ukv", 1))
            dve.wait_ge(panel_used, nth("ukv", 1) + 1)
            for b in range(4):
                t, q = b // 2, b % 2
                dve.wait_ge(s("v_copied"), b + 1)
                v = ps[b][:, :].rearrange("p (h c) -> p h c", c=NOPE + MV)
                line(V.tensor_scalar(k_tm[:, t, 4 * q:4 * q + 4, 0:NOPE], v[:, :, 0:NOPE], invkv[:, t:t + 1], None, mult),
                     "k_copied")

            arrived(dve, "in_mask")
            dve.wait_ge(s("bias_in"), 32)

            def scores(g):
                kind, h = ALL[g]
                dve.wait_ge(s("s_done"), g + 1)
                if g >= 2:
                    dve.wait_ge(s("pt_done"), g - 1)
                if kind == "C":
                    b = bias[:, A_HEADS + h, :]
                    src = [ps[g % 2][:, 0:NCMP0], ps[g % 2][:, P:P + NCMP]]
                    near = CMP_LEN - 1
                    ins = [b[:, SEQ + near:FW:CMP_STRIDE], b[:, P + near:FW:CMP_STRIDE]]
                else:
                    b = {"A": bias[:, h, :], "M": mask[:, :], "F": dec[:, h % FOX_HEADS, :]}.get(
                        kind, bias[:, A_HEADS + h % NSA_HEADS, :])
                    src = [ps[g % 2][:, 0:P], ps[g % 2][:, P:FW]]
                    ins = [b[:, 0:P], b[:, P:FW]]
                for t, z in enumerate(z_parts(g)):
                    line(V.tensor_tensor_reduce(out=z, in0=src[t], in1=ins[t], scale=M_SCALE if kind == "M" else SCALE,
                                                scalar=-3e38, op0=add, op1=ALU.max, accum_out=pair(mx, g)[:, t:t + 1]))
                line.settle()
                line(V.tensor_scalar(pair(nm, g), pair(mx, g), -1.0, None, mult), "z_ready")

            def probabilities(g):
                kind, h = ALL[g]
                dve.wait_ge(s("e_ready"), 2 * (g + 1))
                line(V.reciprocal(pair(rec, g), pair(den, g)))
                line.settle()
                if kind == "C":
                    line(V.tensor_scalar(pair(mx, g), pair(mx, g), NEG / 100, None, ALU.is_gt))
                    line.settle()
                    line(V.tensor_tensor(pair(rec, g), pair(rec, g), pair(mx, g), mult))
                    line.settle()
                if kind in "SWC":
                    b = 4 * "CSW".index(kind) + h
                    line(V.tensor_tensor(pair(rec, g), pair(rec, g), gate2[:, :, b:b + 1].rearrange("p t a -> p (t a)"), mult))
                    line.settle()
                for t, z in enumerate(z_parts(g)):
                    line(V.tensor_scalar(z, z, pair(rec, g)[:, t:t + 1], None, mult), "p_ready")

            for g in range(N1 + 2):
                if g < N1:
                    scores(g)
                    split.ahead(nth("gate", g))
                if 1 <= g <= N1:
                    probabilities(g - 1)
                if g < N1:
                    for m in ADA_JOB[g]:
                        if m == 4 * KC:
                            dve.wait_ge(s("mod_sum"), 3)
                        ada(m)
                if g >= 2:
                    o = OUT[g - 2]
                    dve.wait_ge(s("o_hi"), o + 1)
                    line(V.tensor_tensor(o_rows(mix_lo, o), o_region(o), o_rows(mix_hi, o).bitcast(f32), sub), "o_lo")
            modulate(2, 3)
            line(stt(out=gs[:, 1, :], in0=mod[:, 4, :], scalar=1.0, in1=vb[:, 0:8], op0=add, op1=mult))
            split.ahead(nth("up", 0))
            for c, l in enumerate(L["up"]):
                split.ahead(outputs[l])
                await_out(dve, l)
                dve.wait_ge(s("sig_done"), 2 * c + 2)
                line(V.tensor_tensor(gates[:, c, :], lin(l), gates[:, c, :], mult))
                line(V.tensor_tensor(gates[:, 8 + c, :], lin(l, SEQ, SEQ), gates[:, 8 + c, :], mult), free_name(l))
                if c % 2:
                    ada(ADA_LAST + c // 2)
            for c, l in enumerate(L["wo"]):
                split.ahead(outputs[l])
                await_out(dve, l)
                line(stt(out=xT[:, c, :], in0=lin(l), scalar=mod[:, 2, c:c + 1], in1=xT[:, c, :], op0=mult, op1=add),
                     "x_ready")
                if c < KC // 2:
                    ada(ADA_LAST + KC // 2 + c)
                if c >= 1:
                    total(c - 1, 1)
            total(KC - 1, 1)
            inverse(1)
            normed(1, gs[:, 1, :], 3)
            modulate(5)

            def ffn(f):
                m0 = nth("ffn%d" % f)

                def hidden(j, i, more):
                    J = FC * f + j
                    for m in more[:1]:
                        split_lo(m, i)
                    dve.wait_ge(s("silu_done"), J + 1 + i * 2)
                    line(V.tensor_tensor(hf[:, j % 2, :], sg[:, j % 2, :], bank_of(f, j)[:, SEQ:512], mult), "hf_done")
                    for m in more[1:2]:
                        split_lo(m, i)
                    dve.wait_ge(s("g_hi"), J + 1 + i * 2)
                    line(V.tensor_tensor(g_lo[:, j % 2, :], hf[:, j % 2, :], g_hi[:, j % 2, :].bitcast(f32), sub), "g_lo")
                    for m in more[2:]:
                        split_lo(m, i)
                assert split.next == m0 + AHEAD
                e = split.next
                hidden(0, 0, [e, e + 1])
                for j in (1, 2):
                    hidden(j, 0, [e + 3 * j - 1 + k for k in range(3)])
                with dve.Fori(0, ITER) as i:
                    for j in (3, 4):
                        hidden(j, i, [e + 3 * j - 1 + k for k in range(3)])
                line.skip("hf_done", 2 * (ITER - 1))
                line.skip("g_lo", 2 * (ITER - 1))
                split.next = e + 3 * FC - 4
                more = [m for m in range(split.next, split.next + 3) if m < NS]
                hidden(FC - 1, 0, more)
                split.next += len(more)
                dve.wait_ge(panel_used, m0 + 3 * FC)
                for c in range(KC):
                    acc = ps[c // 2][:, SEQ * (c % 2):SEQ * (c % 2) + SEQ]
                    if f == 0:
                        line(stt(out=xT[:, c, :], in0=acc, scalar=mod[:, 5, c:c + 1], in1=xT[:, c, :], op0=mult,
                                 op1=add), "x_ready")
                        if c >= 2:
                            total(c - 2, 2)
                    else:
                        line(V.tensor_tensor(xT[:, c, :], acc, xT[:, c, :], add), "x_ready")
            ffn(0)
            for c in (KC - 2, KC - 1):
                total(c, 2)
            inverse(2)
            line.settle()
            line(V.tensor_tensor(ms2, NSUM2, inv, mult))
            line.settle()
            line(V.tensor_tensor(ms2, ms2, inv, mult), "ms2_ready")
            dve.wait_ge(s("rms2_ready"), 1)
            line(V.reciprocal(inv2, rms2))
            line.settle()
            line(V.tensor_tensor(inv2, inv2, inv, mult), "inv2_col")
            normed(2, gg)
            for c in range(KC):
                dve.wait_ge(s("h_ready"), 24)
                line(stt(out=xT[:, c, :], in0=xT[:, c, :], scalar=vcol("g_final", c), in1=NRM2, op0=mult,
                         op1=mult), "x_ready")

            split.ahead(nth("fq", 0))
            dve.wait_ge(s("lam_exp"), 1)
            e_, s_, s2, acc_, t_ = spt[0], spt[1], spt[2], spt[3], spt[4]
            line(V.tensor_scalar(t_, e_, 2.0, None, add))
            line.settle()
            line(V.reciprocal(t_, t_))
            line.settle()
            line(V.tensor_tensor(s_, e_, t_, mult))
            line.settle()
            line(V.tensor_tensor(s2, s_, s_, mult))
            line(V.memset(acc_, 1.0 / 15))
            for k in (13, 11, 9, 7, 5, 3, 1):
                line.settle()
                line(V.tensor_tensor(acc_, acc_, s2, mult))
                line.settle()
                line(V.tensor_scalar(acc_, acc_, 1.0 / k, None, add))
            line.settle()
            line(stt(out=acc_, in0=acc_, scalar=2.0, in1=s_, op0=mult, op1=mult))
            line.settle()
            line(V.tensor_scalar(t_, vcol("lru_lambda_2", 0, 2), -1.0, 0.0, mult, ALU.max))
            line.settle()
            line(V.tensor_tensor(acc_, acc_, t_, add))
            line.settle()
            line(V.tensor_scalar(spt[7], acc_, 8.0, None, mult))
            line(V.tensor_scalar(spt[6], acc_, -8.0, None, mult), "lru_c")
            for name in ("kskw", "fg", "vsvw"):
                split.ahead(nth(name))
            split.ahead(nth("fv", 1))
            dve.wait_ge(s("qk_rms"), 1)
            line(V.reciprocal(rinv, rinv), "qk_inv")
            split.ahead(nth("fill", 0))
            arrived(dve, "in_b2")
            dve.wait_ge(s("f_t"), 1)
            line(V.tensor_scalar(cf[:, 0, :], ps[6][0:FOX_HEADS, 0:SEQ], fbias, None, add))
            line.settle()
            line(stt(out=cf[:, 1, :], in0=cf[:, 0, :], scalar=-1.0, in1=cf[:, 0, :], op0=mult, op1=ALU.max), "f_abs")
            line(V.tensor_scalar(cf[:, 0, :], cf[:, 0, :], 0.0, None, ALU.min))
            line(V.tensor_tensor(gate2, fg[:, :, 4:16], gb_row.unsqueeze(1).to_broadcast([P, TT, 12]), add), "gate_sum")
            split.ahead(nth("fill", 1))
            for q, (_, _, dst, gain) in enumerate(QK2):
                dve.wait_ge(s("qk_fac"), q + 1)
                line(stt(out=dst, in0=dst, scalar=vcol(gain), in1=ps[q % 4][:, 0:SEQ], op0=mult, op1=mult), "qk_ready")
            split.ahead(nth("fill", 3))

            dve.wait_ge(s("pads"), 1)

            def conv(dst, src, taps, name, first, c, tell=None):
                for k in range(taps):
                    tap = vcol(name, 2 * k + c)
                    x = src[:, c, k:k + SEQ]
                    if k == 0:
                        line(V.tensor_scalar(dst, x, tap, None, mult) if first is None
                             else V.tensor_scalar(dst, x, tap, first, mult, add))
                    else:
                        line(stt(out=dst, in0=x, scalar=tap, in1=dst, op0=mult, op1=add),
                             tell if k == taps - 1 else None)
                    line.settle()
            for c in range(2):
                l = L["fill"][c]
                dve.wait_ge(s(free_name(l)), freed[l][1])
                conv(xc[:, c, :], lx, 4, "lru_conv_w_2", vcol("lru_conv_b_2", c), c, "xc_ready")
            dve.wait_ge(s("f_log"), 1)
            line(V.tensor_tensor(cf[:, 1, :], cf[:, 1, :], cf[:, 0, :], sub))
            line.settle()
            line(V.tensor_tensor_scan(cf[:, 2, :], ones[0:FOX_HEADS, :], cf[:, 1, :], 0.0, mult, add))
            line.settle()
            line(V.tensor_scalar(cf[:, 2, :], cf[:, 2, :], 8.0, None, mult), "c_ready")
            dve.wait_ge(s("ccol_mm"), 1)
            line(V.tensor_copy(ccol, ps[6][:, 304:312]))
            line.settle()
            for h in range(FOX_HEADS):
                dve.wait_ge(s("crow_mm"), 2 * (h // 2) + 2)
                row = ps[2 + h // 2][:, SEQ * (h % 2):SEQ * (h % 2) + SEQ]
                line(stt(out=dec[:, h, 0:P], in0=row[:, 0:P], scalar=ccol[:, h:h + 1], in1=mask[:, 0:P],
                         op0=sub, op1=add))
                line(stt(out=dec[:, h, P:FW], in0=row, scalar=ccol[:, 4 + h:5 + h], in1=mask[:, P:FW],
                         op0=sub, op1=add), "dec_ready")
            dve.wait_ge(s("kc_rms"), 1)
            line(V.reciprocal(kcq[:, 0:NCMP], kcq[:, 0:NCMP]))
            line.settle()
            line(stt(out=kcT[:, 0:NCMP], in0=kcT[:, 0:NCMP], scalar=vcol("nsa_kc"), in1=kcq[:, 0:NCMP], op0=mult,
                     op1=mult), "kc_ready")

            dve.wait_ge(s("gate2_ready"), 1)
            for g in range(N1, N1 + N2 + 1):
                q = EARLY + g - N1
                if g < N1 + N2:
                    scores(g)
                if q < len(FILL):
                    split.ahead(nth("fill", q))
                if g > N1:
                    probabilities(g - 1)
                if g == N1 + 7:
                    for c in range(2):
                        l = L["fill"][6 + c]
                        dve.wait_ge(s(free_name(l)), freed[l][1])
                    for c in range(2):
                        line(V.tensor_tensor(sx[:, c, 2:], sx[:, c, 2:], s_c[:, c, :], mult))
                        line.settle()
                        conv(s_c[:, c, :], sx, 3, "sc_conv_w_2", None, c)
                        line(V.tensor_tensor(yT[:, 2 + c, :], s_b[:, c, :], s_c[:, c, :], mult),
                             None if c == 0 else "yb_ready")
                if g == N1 + 6:
                    dve.wait_ge(s("lru_sig"), 4)
                    line(V.tensor_tensor(ia, ia, xc, mult))
                    dve.wait_ge(s("lru_tanh"), 2)
                    line.settle()
                    line(V.tensor_scalar(xc, yT[:, 0:2, :], 1.0, None, add))
                    line.settle()
                if N1 + 8 <= g < N1 + 12:
                    x = g - N1 - 8
                    v = xc[:, x // 2, P * (x % 2):P * (x % 2) + P]
                    line.settle()
                    line(V.reciprocal(v, v))
            line.settle()
            line(stt(out=yT[:, 0:2, :], in0=yT[:, 0:2, :], scalar=2.0, in1=xc, op0=mult, op1=mult), "lru_w")
            split.ahead(nth("wout", 0) - 1)
            dve.wait_ge(s("lru_sqrt"), 1)
            line(V.tensor_tensor(ia, ia, yT[:, 0:2, :], mult))
            line.settle()
            for c in range(2):
                line(V.tensor_tensor_scan(xc[:, c, :], ra[:, c, :], ia[:, c, :], 0.0, mult, add))
            line.settle()
            dve.wait_ge(s("lg_ready"), 1)
            line(V.tensor_tensor(yT[:, 0:2, :], xc, lg, mult), "ya_ready")
            for n in range(4):
                c = Y_ORDER[2 * n]
                dve.wait_ge(s("y_sq"), 2 * n + 2)
                line(V.tensor_tensor(sq[:, c, :], sq[:, c, :], sq[:, c + 1, :], add), "y_tot")
            dve.wait_ge(s("y_rms"), 1)
            line(V.reciprocal(yrms, yrms), "y_inv")
            for n in range(KC + 2):
                if n < KC:
                    c = Y_ORDER[n]
                    dve.wait_ge(s("y_fac"), n // 2 + 1)
                    line(stt(out=yT[:, c, :], in0=yT[:, c, :], scalar=vcol("out_norm_2", c), in1=ps[n // 2][:, 0:SEQ],
                             op0=mult, op1=mult), "y_ready")
                if n >= 2:
                    c = Y_ORDER[n - 2]
                    dve.wait_ge(s("y_hi"), n - 1)
                    line(V.tensor_tensor(mix_lo[:, c, :], yT[:, c, :], mix_hi[:, c, :].bitcast(f32), sub), "y_lo")
            for c, l in enumerate(L["wout"]):
                split.ahead(outputs[l])
                await_out(dve, l)
                line(V.tensor_tensor(xT[:, c, :], lin(l), xT[:, c, :], add), "x_ready")
                if c >= 1:
                    total(c - 1, 3)
            total(KC - 1, 3)
            inverse(3)
            normed(3, vcol("norm_ffn_2", 0, 8))
            ffn(1)

        @block.gpsimd
        def _(pool):
            G = nc.gpsimd
            line = Line(pool, "pool_step")

            def rotate(x, h, tell=None):
                a, b = x[:, :, :, 0:HALF], x[:, :, :, HALF:ROPE]
                t = [r[:, :, 0:h, :] for r in rt]
                co = cosT[:, :, :].unsqueeze(2).to_broadcast([P, TT, h, HALF])
                si = sinT[:, :, :].unsqueeze(2).to_broadcast([P, TT, h, HALF])
                for dst, x_, y_ in ((t[0], a, co), (t[1], b, si), (t[2], a, si), (t[3], b, co)):
                    line(G.tensor_tensor(dst, x_, y_, mult))
                line.settle()
                line(G.tensor_tensor(a, t[0], t[1], sub))
                line(G.tensor_tensor(b, t[2], t[3], add), tell)
                line.settle()
            for name in ("in_rel", "in_pos", "in_vb", "in_mask"):
                for dst, src in loads[name]:
                    pool.dma_start(dst, src).then_inc(s(name), 16)
            pool.wait_ge(s("trig_ready"), 1)
            l = L["kr"][0]
            pool.wait_ge(s(free_name(l)), freed[l][1])
            rotate(kr, 1)
            line(G.tensor_copy(k_tm[:, :, :, NOPE:MQ], kr.to_broadcast([P, TT, MH, ROPE])), "rope_k")
            pool.wait_ge(s("q_copied"), 4)
            rotate(q_tm[:, :, :, NOPE:MQ], MH, "rope_q")
            for c, l in enumerate(L["up"]):
                pool.wait_ge(s(free_name(l)), freed[l][1])
                line(G.tensor_tensor(sq[:, c, :], gates[:, c, :], gates[:, 8 + c, :], add), "merged")
                pool.wait_ge(s("m_hi"), c + 1)
                line(G.tensor_tensor(h_lo[:, c, :], sq[:, c, :], h_hi[:, c, :].bitcast(f32), sub), "m_lo")
            line(G.memset(lw, 0.0))
            line(G.memset(lx[:, :, 0:3], 0.0))
            line(G.memset(sx[:, :, 0:2], 0.0), "pads")
            line.settle()
            for name, group in loads2.items():
                for dst, src in group:
                    pool.dma_start(dst, src).then_inc(s(name), 16)
            for c in range(1, KC):
                pool.wait_ge(s("sqg_ready"), c + 1)
                if c > 1:
                    line.settle()
                line(G.tensor_tensor(totg[:, :], sqg[:, 0, :] if c == 1 else totg[:, :], sqg[:, c, :], add),
                     "totg_ready" if c == KC - 1 else None)
            l = L["kcvc"][0]
            pool.wait_ge(s(free_name(l)), freed[l][1])
            for a in (0, HD):
                pool.dma_start(kcvc_x[a:a + HD, :], kcvc[HD - a:2 * HD - a, :]).then_inc(s("kcvc_x_in"), 16)
            pool.wait_ge(s("kcvc_x_in"), 32)
            for kv, lower, upper in ((0, kcvc, kcvc_x), (1, kcvc_x, kcvc)):
                for e, x in ((0, lower), (1, upper)):
                    r = slice(HD * e, HD * e + HD)
                    x16 = x[r, :].rearrange("p (n s) -> p s n", s=CMP_STRIDE)
                    for n in range(CMP_LEN // CMP_STRIDE):
                        k0 = VB["pos"] + 16 * kv + 8 * n
                        pos = vb[r, k0:k0 + 8].unsqueeze(2).to_broadcast([HD, 8, NCMP])
                        last = kv == 1 and e == 1 and n == 1
                        line(G.tensor_tensor(xb[r, kv, 8 * n:8 * n + 8, :], x16[:, e:CMP_STRIDE:2, n:n + NCMP], pos, add),
                             "xb_ready" if last else None)
            pool.wait_ge(s("qk_ready"), 7)
            for a in (0, HD):
                pool.dma_start(kskw_x[a:a + HD, :], kskw[HD - a:2 * HD - a, :]).then_inc(s("kskw_x_in"), 16)

        @block.tensor
        def _(pe):
            T = nc.tensor
            line = Line(pe, "pe_step")

            def product(dst, stat, mov, start, stop, shared=False):
                kw = {"skip_group_check": True} if shared else {}
                T.matmul(dst, stat[0], mov[0], start=start, stop=False, **kw)
                T.matmul(dst, stat[0], mov[1], start=False, stop=False, **kw)
                return T.matmul(dst, stat[1], mov[0], start=False, stop=stop, **kw)

            def hx(c):
                return h_hi[:, c, :], h_lo[:, c, :]

            def mxp(c):
                return mix_hi[:, c, :], mix_lo[:, c, :]

            def await_split(m, i=0):
                pe.wait_ge(lo_done, m + 1 + i * 6)

            def await_bank(l):
                if l >= 2:
                    name, v = freed[l - 2]
                    pe.wait_ge(s(name), v)

            def chunk_out(l, act, fresh=None, order=range(KC)):
                m = outputs[l]
                await_split(m)
                await_bank(l)
                for n, k in enumerate(order):
                    if fresh is not None:
                        pe.wait_ge(s(fresh[0]), fresh[1] + n + 1)
                    ins = product(lin(l), hi_lo(m, k * P, P), act(k), n == 0, n == KC - 1)
                ins.then_inc(panel_used, 1)

            def tokens_out(ls, ms, kn, n):
                for l in ls:
                    await_bank(l)
                for x, m in enumerate(ms):
                    await_split(m)
                    for k in range(kn):
                        a = hx(x * kn + k)
                        for t, l in enumerate(ls):
                            ins = product(lin(l, n), [v[:, t * P:(t + 1) * P] for v in a], hi_lo(m, k * n, n),
                                          x == 0 and k == 0, x == len(ms) - 1 and k == kn - 1)
                    ins.then_inc(panel_used, 1)

            def ada_sum(g):
                pe.wait_ge(ada_used, KC * (g + 1))
                for c in range(KC):
                    ins = T.matmul(MOD[:, KC * g + c:KC * g + c + 1], ada_acc(g)[:, c * P:(c + 1) * P], ones[:, 0:1],
                                   start=True, stop=True)
                line(ins, "mod_sum")

            arrived(pe, "in_id")
            arrived(pe, "in_va")
            line(T.transpose(ps[5][:, 0:VA_ROWS], va_rows, ident[0:VA_ROWS, 0:VA_ROWS]), "va_t")
            arrived(pe, "in_x")
            for b in range(4):
                for q in range(4):
                    c, t = 2 * b + q // 2, q % 2
                    ins = T.transpose(ps[b][:, q * P:(q + 1) * P], x_tm[:, t, c * P:(c + 1) * P], ident[:, :])
                line(ins, "x_t")
            def by_token(dst, src):
                for t in range(TT):
                    ins = T.matmul(dst[:, t:t + 1], src[:, t * P:(t + 1) * P], ones[:, 0:1], start=True, stop=True)
                return ins

            def sums(k):
                pe.wait_ge(s("tot_ready"), k + 1)
                ins = by_token(NSUM, tot)
                if k == 2:
                    pe.wait_ge(s("totg_ready"), 1)
                    ins = by_token(NSUM2, totg)
                line(ins, "ss_done")

            def spread(dst, v):
                for t in range(TT):
                    ins = T.matmul(dst[:, t * P:(t + 1) * P], v[:, t:t + 1].to_broadcast([P, P]), ident[:, :],
                                   start=True, stop=True)
                return ins

            def factor(k):
                if k == 2:
                    pe.wait_ge(s("inv2_col"), 1)
                    spread(NRM2, inv)
                    line(spread(NRM, inv2), "inv_ready")
                else:
                    pe.wait_ge(s("inv_col"), k + 1)
                    line(spread(NRM, inv), "inv_ready")
            pe.wait_ge(s("const_ready"), 1)
            sums(0)
            arrived(pe, "in_rel")
            pe.wait_ge(s("x_copied"), 4)
            for n, (h0, h1) in enumerate(((0, A_HEADS), (A_HEADS, NB))):
                line(T.matmul(ps[n][0:h1 - h0, 0:FW], relc[:, h0:h1], onehot[:, n, :], start=True, stop=True), "frow_mm")
            ada_sum(0)
            factor(0)
            arrived(pe, "in_vb")
            line(T.transpose(ps[2][:, 0:VB_ROWS], vb_rows[0:VB_ROWS], ident[0:VB_ROWS, 0:VB_ROWS]), "vb_t")
            ada_sum(1)

            for l in L["cq"] + L["ckv"]:
                chunk_out(l, hx, fresh=("h_lo", 0) if l == L["cq"][0] else None)
            m, l = nth("kr"), L["kr"][0]
            await_split(m)
            await_bank(l)
            for t in range(TT):
                for k in range(KC):
                    ins = product(lin(l, ROPE, ROPE * t), [v[:, t * P:(t + 1) * P] for v in hx(k)],
                                  hi_lo(m, k * ROPE, ROPE), k == 0, k == KC - 1)
            ins.then_inc(panel_used, 1)
            for l in L["aq"] + L["ak"]:
                chunk_out(l, hx)
            tokens_out(L["av"], [nth("av", k) for k in range(4)], 2, AW)
            pe.wait_ge(s("lat_sq"), 8)
            pe.wait_ge(s("vb_ready"), 1)
            for t in range(TT):
                for q, (c0, c1) in enumerate(((0, 6), (6, 8))):
                    for c in range(c0, c1):
                        ins = T.matmul(ps[7][:, 2 * q + t:2 * q + t + 1], sq[:, c, t * P:(t + 1) * P], ones[:, 0:1],
                                       start=(c == c0), stop=(c == c1 - 1))
            line(ins, "lat_ss")
            pe.wait_ge(s("frow_copied"), 2)
            for name, kn, n, c0 in (("uq", 6, 384, 0), ("ukv", 2, 512, 6)):
                for k in range(kn):
                    m = nth(name, k)
                    await_split(m)
                    if name == "ukv" and k == 0:
                        pe.wait_ge(s("q_copied"), 4)
                    for b in range(4):
                        t, q = b // 2, b % 2
                        ins = product(ps[b][:, 0:n], [v[:, t * P:(t + 1) * P] for v in mxp(c0 + k)],
                                      hi_lo(m, q * n, n), k == 0, k == kn - 1)
                    ins.then_inc(panel_used, 1)

            def qk_turn(h):
                if h >= 1:
                    pe.wait_ge(s("qk_copied"), h)
                for x, src in enumerate((q_tm, k_tm)):
                    for t in range(TT):
                        ins = T.transpose(ps[3][0:MQ, (2 * x + t) * P:(2 * x + t + 1) * P], src[:, t, h, :], ident[:, :])
                line(ins, "qkt_done")

            def make_scores(g):
                kind, h = ALL[g]
                if g >= 2:
                    pe.wait_ge(s("z_ready"), g - 1)
                r = slice(HD * (h % 2), HD * (h % 2) + HD)
                if kind == "A":
                    q, k = aqT[r, h // 2, :], akT[r, h // 2, :]
                elif kind == "M":
                    pe.wait_ge(s("qk_copied"), h + 1)
                    q, k = [qkb[:, 2 * x:2 * x + 2, :].rearrange("p a b -> p (a b)") for x in range(2)]
                elif kind == "F":
                    q, k = fqT[r, h // 2, :], fkT[r, h // 2, :]
                else:
                    q = nqT[r, h // 2, :]
                    own, other = kskw[r, :], kskw_x[r, :]
                    k = {"S": (own, other)[h % 2], "W": (other, own)[h % 2], "C": kcT[r, :]}[kind]
                if kind == "C":
                    T.matmul(ps[g % 2][:, 0:NCMP0], q[:, 0:P], k[:, 0:NCMP0], start=True, stop=True)
                    ins = T.matmul(ps[g % 2][:, P:P + NCMP], q[:, P:SEQ], k[:, 0:NCMP], start=True, stop=True)
                else:
                    T.matmul(ps[g % 2][:, 0:P], q[:, 0:P], k[:, 0:P], start=True, stop=True)
                    ins = T.matmul(ps[g % 2][:, P:FW], q[:, P:SEQ], k[:, 0:SEQ], start=True, stop=True)
                line(ins, "s_done")

            def turn(g):
                pe.wait_ge(s("p_ready"), 2 * (g + 1))
                if g >= 1:
                    pe.wait_ge(s("pt_copied"), g)
                if ALL[g][0] == "C":
                    for t in range(TT):
                        ins = T.transpose(ps[2][0:NCMP, t * P:(t + 1) * P], zc[:, g % 2, t, 0:NCMP], ident[:, :])
                else:
                    for b in range(3):
                        ins = T.transpose(ps[2][:, b * P:(b + 1) * P], zb[:, g % 2, b * P:(b + 1) * P], ident[:, :])
                line(ins, "pt_done")

            def gather(g):
                kind, h = ALL[g]
                o = OUT[g]
                pe.wait_ge(s("pt_copied"), g + 1)
                if o >= 2 and OUT[g - 1] != o:
                    pe.wait_ge(s("o_lo" if o - 2 < 16 else "o_hi"), o - 1)
                dst = o_region(o)
                first = kind in "AMFS"
                if kind == "C":
                    ins = T.matmul(dst, v_c[0:NCMP, :], ptb[0:NCMP, g % 2, 0:SEQ], start=False, stop=True,
                                   skip_group_check=True)
                else:
                    v = {"A": lambda t: a_v[:, t, HD * h:HD * h + HD], "M": lambda t: m_v[:, t, HD * h:HD * h + HD],
                         "F": lambda t: f_v[:, t, HD * h:HD * h + HD], "S": lambda t: n_v[:, t, 0, :],
                         "W": lambda t: n_v[:, t, 1, :]}[kind]
                    T.matmul(dst, v(0), ptb[:, g % 2, 0:SEQ], start=first, stop=False, skip_group_check=True)
                    ins = T.matmul(dst[:, P:SEQ], v(1), ptb[:, g % 2, SEQ:FW], start=False, stop=True,
                                   skip_group_check=True)
                line(ins, "pv_done")

            pe.wait_ge(s("v_copied"), 4)
            pe.wait_ge(s("k_copied"), 4)
            pe.wait_ge(s("bias_in"), 32)
            make_scores(0)
            for g in range(N1 + 2):
                if g + 1 < N1:
                    make_scores(g + 1)
                if g + 2 == A_HEADS:
                    pe.wait_ge(s("rope_q"), 1)
                if A_HEADS <= g + 2 < N1:
                    qk_turn(g + 2 - A_HEADS)
                if g < N1:
                    chunk_out(L["gate"][g], hx)
                if 1 <= g <= N1:
                    turn(g - 1)
                if g >= 2:
                    gather(g - 2)
                if g in ADA_SUM:
                    ada_sum(ADA_SUM[g])
            pe.wait_ge(s("o_lo"), 16)
            for c, l in enumerate(L["up"]):
                m = outputs[l]
                await_split(m)
                await_bank(l)
                for x in range(2):
                    for k in range(4):
                        ins = product(lin(l, SEQ, SEQ * x), hi_lo(m, (4 * x + k) * P, P), mxp(4 * x + k), k == 0, k == 3)
                ins.then_inc(panel_used, 1)
            for l in L["wo"]:
                chunk_out(l, hx, fresh=("m_lo", 0) if l == L["wo"][0] else None)
            sums(1)
            factor(1)
            ada_sum(5)

            def ffn(f):
                m0 = nth("ffn%d" % f)
                def gate_up(j, i=0):
                    J = FC * f + j
                    if j >= 2:
                        pe.wait_ge(s("hf_done"), J - 1 + i * 2)
                    for x, what in enumerate("gu"):
                        m = m0 + f_pos(what, j)
                        await_split(m, i)
                        for k in range(KC):
                            if j == 0 and x == 0:
                                pe.wait_ge(s("h_lo"), 8 + 16 * f + k + 1)
                            ins = product(bank_of(f, j)[:, SEQ * x:SEQ * x + SEQ], hi_lo(m, k * P, P), hx(k), k == 0,
                                          k == KC - 1)
                        ins.then_inc(panel_used, 1)

                def down(j, i=0):
                    J = FC * f + j
                    m = m0 + f_pos("d", j)
                    await_split(m, i)
                    pe.wait_ge(s("g_lo"), J + 1 + i * 2)
                    for c in range(KC):
                        ins = product(ps[c // 2][:, SEQ * (c % 2):SEQ * (c % 2) + SEQ], hi_lo(m, c * P, P),
                                      (g_hi[:, j % 2, :], g_lo[:, j % 2, :]), j == 0 and c % 2 == 0, j == FC - 1,
                                      shared=True)
                    ins.then_inc(panel_used, 1)
                gate_up(0)
                for j in (1, 2):
                    gate_up(j)
                    down(j - 1)
                with pe.Fori(0, ITER) as i:
                    for j in (3, 4):
                        gate_up(j, i)
                        down(j - 1, i)
                gate_up(FC - 1)
                down(FC - 2)
                down(FC - 1)
            ffn(0)
            sums(2)
            factor(2)

            for l in L["fq"] + L["fk"] + L["nq"] + L["kcvc"] + L["kskw"]:
                chunk_out(l, hx, fresh=("h_lo", 16) if l == L["fq"][0] else None)
            for name, n in (("fg", 16), ("vsvw", P)):
                m, l = nth(name), L[name][0]
                await_split(m)
                await_bank(l)
                for t in range(TT):
                    for k in range(KC):
                        ins = product(lin(l, n, n * t), [v[:, t * P:(t + 1) * P] for v in hx(k)],
                                      hi_lo(m, k * n, n), k == 0, k == KC - 1)
                ins.then_inc(panel_used, 1)
            tokens_out(L["fv"], [nth("fv", k) for k in range(2)], 4, GROUP)
            arrived(pe, "in_heads")
            for q in range(7):
                pe.wait_ge(s("qk_sq"), q + 1)
                a = NROW - 2 - 2 * q
                ins = T.matmul(ps[0][0:NROW, 0:SEQ], heads[:, a:a + NROW], sq[:, q, :], start=(q == 0), stop=(q == 6))
            line(ins, "qk_ss")
            l = L["fg"][0]
            pe.wait_ge(s(free_name(l)), freed[l][1])
            for t in range(TT):
                ins = T.transpose(ps[6][0:FOX_HEADS, t * P:(t + 1) * P], fg[:, t, 0:FOX_HEADS], ident[:, :])
            line(ins, "f_t")
            for l in L["fill"][:EARLY]:
                chunk_out(l, hx)
                if l == L["fill"][1]:
                    pe.wait_ge(s("qk_inv"), 1)
                    for q in range(7):
                        if q >= 4:
                            pe.wait_ge(s("qk_ready"), q - 3)
                        line(T.matmul(ps[q % 4][:, 0:SEQ], rows14[:, q * P:(q + 1) * P], rinv, start=True, stop=True),
                             "qk_fac")
            pe.wait_ge(s("xb_ready"), 1)
            for kv in range(2):
                for half in range(2):
                    m = ADA + 2 * kv + half
                    n = direct_of[m]
                    pe.wait_ge(raw_in[n % RAW], raw_count[n])
                    for k in range(8):
                        last = T.matmul(ps[7][:, 16 * kv:16 * kv + NCMP], raw[:, n % RAW, k * P:(k + 1) * P],
                                        xb[:, kv, 8 * half + k, :], start=(half == 0 and k == 0),
                                        stop=(half == 1 and k == 7))
                    last.then_inc(cmp_used, 1)
            pe.wait_ge(s("c_ready"), 1)
            arrived(pe, "in_b2")
            for t in range(TT):
                ins = T.matmul(ps[6][:, 304 + 4 * t:308 + 4 * t], cf[:, 2, t * P:(t + 1) * P], ident[0:FOX_HEADS, 0:FOX_HEADS],
                               start=True, stop=True)
            line(ins, "ccol_mm")
            pe.wait_ge(s("qk_ready"), 7)
            for h in range(FOX_HEADS):
                line(T.matmul(ps[2 + h // 2][:, SEQ * (h % 2):SEQ * (h % 2) + SEQ], selb[:, h, :], cf[:, 2, :],
                              start=True, stop=True), "crow_mm")
            arrived(pe, "in_lw")
            pe.wait_ge(s("xc_ready"), 2)
            for q in range(4):
                g, c = q // 2, q % 2
                line(T.matmul(ps[g][:, SEQ * c:SEQ * c + SEQ], lw[:, g, c, :], xc[:, c, :], start=True, stop=True),
                     "lru_mm")
            pe.wait_ge(s("hid_ready"), 1)
            pe.wait_ge(s("dec_ready"), 4)
            line(T.matmul(ps[7][:, 32:32 + NCMP], w2k.rearrange("p a b -> p (a b)"), hid[:, 0, 0:NCMP],
                          start=True, stop=True), "kc_mm")
            line(T.matmul(ps[6][0:NCMP, 64:64 + HD], hid[:, 1, 0:NCMP], w2v, start=True, stop=True), "vc_mm")
            pe.wait_ge(s("kc_sq"), 1)
            line(T.matmul(ps[7][:, 48:48 + NCMP], half1[:, :], kcq[:, 0:NCMP], start=True, stop=True), "kc_ss")
            pe.wait_ge(s("qk_ready"), 7)
            pe.wait_ge(s("lru_sig"), 4)
            pe.wait_ge(s("kc_ready"), 1)
            pe.wait_ge(s("vc_ready"), 1)
            make_scores(N1)
            for g in range(N1, N1 + N2 + 2):
                if g + 1 < N1 + N2:
                    if ALL[g + 1] == ("S", 0):
                        pe.wait_ge(s("kskw_x_in"), 32)
                    make_scores(g + 1)
                q = EARLY + g - N1
                if q < len(FILL):
                    chunk_out(L["fill"][q], hx)
                if N1 < g <= N1 + N2:
                    turn(g - 1)
                if g >= N1 + 2:
                    gather(g - 2)
            for n in range(4):
                pe.wait_ge(s("y_tot"), n + 1)
                line(by_token(YSUM[:, 2 * n:2 * n + 2], sq[:, Y_ORDER[2 * n], :]), "y_ss")
            pe.wait_ge(s("y_inv"), 1)
            for n in range(4):
                line(spread(ps[n][:, 0:SEQ], yrms[:, 2 * n:2 * n + 2]), "y_fac")
            for l in L["wout"]:
                chunk_out(l, mxp, fresh=("y_lo", 0) if l == L["wout"][0] else None, order=Y_ORDER)
            sums(3)
            factor(3)
            ffn(1)
            for b in range(4):
                for q in range(4):
                    c = 4 * (b % 2) + q
                    pe.wait_ge(s("x_ready"), 32 + max(c + 1, 2 * b + 2))
                    ins = T.transpose(ps[b][:, q * P:(q + 1) * P], xT[:, c, (b // 2) * P:(b // 2 + 1) * P], ident[:, :])
                line(ins, "y_t")


INPUTS = {"x": (SEQ, D), "c": (D,), "positions": (SEQ,), "rel_bias": (A_HEADS, BUCKETS), "w_ada": (D, 6 * D),
          "b_ada": (6 * D,), "g_mix": (D,), "w_in": (D, -1), "g_q_lora": (Q_LORA,), "w_uq": (Q_LORA, MH * MQ),
          "g_kv_lora": (KV_LORA,), "w_ukv": (KV_LORA, MH * (NOPE + MV)), "w_up_a": (AW, D), "w_up_b": (MH * MV, D),
          "w_o": (D, D), "g_ffn": (D,), "w_gate": (D, D_FF), "w_up": (D, D_FF), "w_down": (D_FF, D), "g_final": (D,),
          "norm_mix_2": (D,), "w_in_2": (D, N_IN2), "lru_conv_w_2": (-1,), "lru_conv_b_2": (-1,),
          "lru_w_gates_2": (2, 4, HD, HD), "lru_b_gates_2": (-1,), "lru_lambda_2": (-1,), "sc_conv_w_2": (-1,),
          "fox_f_bias_2": (FOX_HEADS, 1), "fox_qk_norm_2": (2, HD), "nsa_qk_norm_2": (4, HD), "nsa_cmp_pos_2": (-1,),
          "nsa_cmp_w1_2": (2, CMP_LEN * HD, P), "nsa_cmp_w2_2": (2, P, HD), "nsa_gate_bias_2": (3 * NSA_HEADS,),
          "rel_bias_2": (BUCKETS, NSA_HEADS), "out_norm_2": (D,), "w_out_2": (D, D), "norm_ffn_2": (D,),
          "w_gate_up_2": (D, 2 * D_FF), "w_down_2": (D_FF, D)}


def kernel(**inputs):
    import concourse.bacc as bacc
    from concourse.bass_utils import run_bass_kernel_spmd

    nc = bacc.Bacc("TRN2", target_bir_lowering=False, num_devices=1)
    arrays = {name: np.ascontiguousarray(np.asarray(inputs[name]).reshape(shape)) for name, shape in INPUTS.items()}
    arrays.update(shape_constants())
    aps = {name: nc.dram_tensor(f"in_{name}", a.shape, mybir.dt.from_np(a.dtype), kind="ExternalInput").ap()
           for name, a in arrays.items()}
    out = nc.dram_tensor("out_x", (SEQ, D), mybir.dt.float32, kind="ExternalOutput").ap()
    build(nc, aps, out)
    ran = run_bass_kernel_spmd(nc, [{f"in_{name}": a for name, a in arrays.items()}], core_ids=[0])
    return ran.results[0]["out_x"].reshape(1, SEQ, D)
```
